# Optimizing a Trainium2 kernel written in Bass

```python
import jax, jax.numpy as jnp
from jax import lax
import numpy as np

D_MODEL = 1024
BATCH = 1
SEQ = 1024
DEPTH = 1

CHUNK = 64
N_LEFT_CHUNKS = 8
BAND_CHUNKS = N_LEFT_CHUNKS + 1
BAND = BAND_CHUNKS * CHUNK
LEFT_PAD = N_LEFT_CHUNKS * CHUNK
MIX_WIDTH = D_MODEL
CONV_WIDTH = MIX_WIDTH // 2
ATTN_WIDTH = MIX_WIDTH - CONV_WIDTH
HEAD_DIM = 64
N_HEADS = ATTN_WIDTH // HEAD_DIM
CONV_GROUPS = 8
CONV_K = 3
REL_CLIP = 128
D_FF = -(-8 * D_MODEL // (3 * 256)) * 256
PROJ_WIDTH = 3 * CONV_WIDTH + 3 * ATTN_WIDTH
EPS = 1e-6
NEG_INF = -1e30

kernel_name = "hybrid_shortconv_chunkattn_sandwich_trunk"

def rms_norm(x, g):
    xf = x.astype(jnp.float32)
    y = xf * lax.rsqrt(jnp.mean(xf * xf, axis=-1, keepdims=True) + EPS)
    return (y * g.astype(jnp.float32)).astype(x.dtype)

def group_rms_norm(y, g, n_groups):
    b, s, w = y.shape
    yf = y.astype(jnp.float32).reshape(b, s, n_groups, w // n_groups)
    yf = yf * lax.rsqrt(jnp.mean(yf * yf, axis=-1, keepdims=True) + EPS)
    return (yf.reshape(b, s, w) * g.astype(jnp.float32)).astype(y.dtype)

def short_gated_conv(h, b_gate, c_gate, w_conv):
    s = h.shape[1]
    u = c_gate * h
    up = jnp.pad(u, ((0, 0), (CONV_K - 1, 0), (0, 0)))
    out = up[:, 0:s] * w_conv[:, 0]
    for k in range(1, CONV_K):
        out = out + up[:, k:k + s] * w_conv[:, k]
    return b_gate * out

def chunked_band_attention(q, k, v, rel_bias):
    b, s, _ = q.shape
    nc = s // CHUNK
    qc = q.reshape(b, nc, CHUNK, N_HEADS, HEAD_DIM) * (HEAD_DIM ** -0.5)
    kp = jnp.pad(k, ((0, 0), (LEFT_PAD, 0), (0, 0))).reshape(b, nc + N_LEFT_CHUNKS, CHUNK, N_HEADS, HEAD_DIM)
    vp = jnp.pad(v, ((0, 0), (LEFT_PAD, 0), (0, 0))).reshape(b, nc + N_LEFT_CHUNKS, CHUNK, N_HEADS, HEAD_DIM)
    kb = jnp.concatenate([kp[:, o:o + nc] for o in range(BAND_CHUNKS)], axis=2)
    vb = jnp.concatenate([vp[:, o:o + nc] for o in range(BAND_CHUNKS)], axis=2)
    scores = jnp.einsum('bcqhd,bckhd->bhcqk', qc, kb).astype(jnp.float32)
    qi = jnp.arange(CHUNK)[:, None]
    kj = jnp.arange(BAND)[None, :]
    rel_idx = jnp.clip(qi - kj + LEFT_PAD, -REL_CLIP, REL_CLIP) + REL_CLIP
    bias = rel_bias.astype(jnp.float32)[:, rel_idx]
    key_pos = jnp.arange(nc)[:, None] * CHUNK - LEFT_PAD + jnp.arange(BAND)[None, :]
    valid = key_pos >= 0
    scores = jnp.where(valid[None, None, :, None, :], scores + bias[None, :, None], NEG_INF)
    p = jax.nn.softmax(scores, axis=-1).astype(v.dtype)
    o = jnp.einsum('bhcqk,bckhd->bcqhd', p, vb)
    return o.reshape(b, s, ATTN_WIDTH)

def setup_inputs(seed: int = 0) -> dict:
    key = jax.random.key(seed)
    ks = jax.random.split(key, 14)
    f32 = jnp.float32

    def gain(k, n):
        return 1.0 + 0.1 * jax.random.normal(k, (DEPTH, n), f32)

    return {
        "x": jax.random.normal(ks[0], (BATCH, SEQ, D_MODEL), f32),
        "w_in": jax.random.normal(ks[1], (DEPTH, D_MODEL, PROJ_WIDTH), f32) * D_MODEL ** -0.5,
        "w_conv": jax.random.normal(ks[2], (DEPTH, CONV_WIDTH, CONV_K), f32) * CONV_K ** -0.5,
        "rel_bias": 0.5 * jax.random.normal(ks[3], (DEPTH, N_HEADS, 2 * REL_CLIP + 1), f32),
        "g_conv_out": gain(ks[4], CONV_WIDTH),
        "g_attn_out": gain(ks[5], ATTN_WIDTH),
        "w_out": jax.random.normal(ks[6], (DEPTH, MIX_WIDTH, D_MODEL), f32) * MIX_WIDTH ** -0.5,
        "g_pre_mix": gain(ks[7], D_MODEL),
        "g_post_mix": gain(ks[8], D_MODEL),
        "g_pre_ffn": gain(ks[9], D_MODEL),
        "g_post_ffn": gain(ks[10], D_MODEL),
        "w_ffn_in": jax.random.normal(ks[11], (DEPTH, D_MODEL, 2 * D_FF), f32) * D_MODEL ** -0.5,
        "w_ffn_out": jax.random.normal(ks[12], (DEPTH, D_FF, D_MODEL), f32) * D_FF ** -0.5,
    }

def reference(x, w_in, w_conv, rel_bias, g_conv_out, g_attn_out, w_out,
              g_pre_mix, g_post_mix, g_pre_ffn, g_post_ffn, w_ffn_in, w_ffn_out):
    for l in range(DEPTH):
        h = rms_norm(x, g_pre_mix[l])
        proj = jnp.einsum('bsd,dp->bsp', h, w_in[l])
        hc, bg, cg, q, k, v = jnp.split(proj, 6, axis=-1)
        y_conv = short_gated_conv(hc, bg, cg, w_conv[l])
        y_attn = chunked_band_attention(q, k, v, rel_bias[l])
        y = jnp.concatenate([group_rms_norm(y_conv, g_conv_out[l], CONV_GROUPS),
                             group_rms_norm(y_attn, g_attn_out[l], N_HEADS)], axis=-1)
        y = jnp.einsum('bsm,md->bsd', y, w_out[l])
        x = x + rms_norm(y, g_post_mix[l])
        h = rms_norm(x, g_pre_ffn[l])
        gate, up = jnp.split(jnp.einsum('bsd,df->bsf', h, w_ffn_in[l]), 2, axis=-1)
        f = jnp.einsum('bsf,fd->bsd', jax.nn.silu(gate) * up, w_ffn_out[l])
        x = x + rms_norm(f, g_post_ffn[l])
    return x


_drawn_inputs = setup_inputs


def setup_inputs(seed=0):
    import zlib

    import numpy as np

    out = dict(_drawn_inputs(seed))
    spreads = {}
    factors = {}
    for name, (base, spread) in spreads.items():
        noise = np.random.default_rng([zlib.crc32(name.encode()), seed]).standard_normal(out[name].shape)
        drawn = base * np.exp(spread * noise) if base else spread * noise
        out[name] = __import__('jax').numpy.asarray(drawn.astype(out[name].dtype))
    for name, factor in factors.items():
        out[name] = (out[name] * factor).astype(out[name].dtype)
    return out
```

```python
from contextlib import ExitStack, contextmanager

import concourse.bass as bass
from concourse import mybir

F32 = mybir.dt.float32
F32R = mybir.dt.float32r
I32 = mybir.dt.int32
ALU = mybir.AluOpType
ACT = mybir.ActivationFunctionType

P = 128
EPS = 1e-6
NEG = -1e30


class Chain:

    def __init__(self, engine, sem):
        self.engine, self.sem, self.count, self.base = engine, sem, 0, 0

    def __call__(self, instruction):
        instruction.then_inc(self.sem, 1)
        self.count += 1
        self.engine.wait_ge(self.sem, self.base + self.count)

    @contextmanager
    def loop(self, i, rounds, per_round):
        before = self.count
        self.base = i * per_round
        yield
        assert self.count - before == per_round, (self.count - before, per_round)
        self.base = 0
        self.count = before + rounds * per_round


def trunk_layer(nc, x, w_in, w_conv, rel_bias, g_conv_out, g_attn_out, w_out, g_pre_mix, g_post_mix,
                g_pre_ffn, g_post_ffn, w_ffn_in, w_ffn_out, out):
    _, SEQ, D = x.shape
    _, CONV, TAPS = w_conv.shape
    _, HEADS, REL = rel_bias.shape
    ATTN = g_attn_out.shape[1]
    FF = w_ffn_out.shape[1]
    HD = ATTN // HEADS
    CLIP = (REL - 1) // 2
    CHUNK = 64
    LEFT = 8 * CHUNK

    NT = SEQ // P
    KT = D // P
    PAIRS = HEADS // 2
    UNITS = 2 * NT
    BAND = LEFT + P
    STEPS = UNITS + 3
    HALF = SEQ // 2
    NF = FF // P
    assert CONV // P == PAIRS and NT == 8 and KT == 8 and HD == 64 and D == SEQ == 1024 and NF == 22

    OUT0 = 6 * PAIRS
    PASSES = [(0, 1, 2), (3, 4, 5), (6, 7)]
    FIN0 = OUT0 + len(PASSES) * KT
    FOUT0 = FIN0 + 2 * NF
    END = FOUT0 + 2 * NF

    x_d, out_d = x[0], out[0]
    win_d = w_in[0].rearrange("(k p) n -> p k n", p=P)
    wout_d = w_out[0]
    fin_d = w_ffn_in[0].rearrange("(k p) n -> p k n", p=P)
    fout_d = w_ffn_out[0]
    x2_d = nc.dram_tensor("x2_scratch", [SEQ, D], F32, kind="Internal").ap()
    ERW = BAND + P - 1
    ext_d = nc.dram_tensor("bias_scratch", [HEADS, ERW], F32, kind="Internal").ap()

    ctx = ExitStack()
    with ctx:
        def sb(name, shape, dt=F32):
            return ctx.enter_context(nc.sbuf_tensor(name, shape, dt))

        def sem(name):
            return ctx.enter_context(nc.semaphore(name))

        hT = sb("hT", [P, 2, KT, SEQ], F32R)
        ws = sb("ws", [P, 4, 2, D], F32R)
        raw = sb("raw", [P, 2, D])
        arena = sb("arena", [P, NF * SEQ])
        misc = sb("misc", [P, 4 * BAND])
        ident = sb("ident", [P, P])
        group = sb("group", [P, 2])
        params = sb("params", [P, PAIRS, 5])
        cur = sb("cur", [P, 5])
        relb = sb("relb", [HEADS, REL])
        nmax = sb("nmax", [P, 2])
        lsum = sb("lsum", [P, 4])
        osq = sb("osq", [P, 2])
        o_raw = sb("o_raw", [P, 2, P])
        ssq = sb("ssq", [P, 32])
        var = sb("var", [P, 16])
        rst = sb("rst", [P, 16])
        newt = sb("newt", [P, 16])
        crs = sb("crs", [P, 16])
        gate = sb("gate", [P, 1])
        sq_junk = sb("sq_junk", [P, HD])
        PP = [ctx.enter_context(nc.psum_tensor(f"pair{n}", [P, 1024], F32)) for n in range(4)]

        def row(n, width=SEQ, at=0):
            return arena[:, n * SEQ + at:n * SEQ + at + width]

        yT = 0
        BIAS = 8
        QN, KN, VN, Q, K, V = 13, 14, 15, 16, 17, 18
        CV, CU, CR = 19, 20, 21
        cu = row(CU, SEQ + TAPS - 1)
        bias = arena[:, BIAS * SEQ:BIAS * SEQ + HEADS * BAND]
        s_sb = [misc[:, n * BAND:(n + 1) * BAND] for n in range(2)]
        pT = [misc[:, (2 + n) * BAND:(3 + n) * BAND] for n in range(2)]
        ext = row(CR, ERW)[0:HEADS, :]
        JUNK = CV
        H_A = (QN, KN)
        GPRE = VN
        YS, XS, GPM, GPF, H_O = (8, 9, 10), (11, 12), 13, 14, (15, 16)
        sil = [misc[:, n * SEQ:(n + 1) * SEQ] for n in range(2)]
        a3 = arena[:, :].rearrange("p (f s) -> p f s", s=SEQ)
        x2t = [a3[:, 2 * n:2 * n + 2, 0:HALF] for n in range(4)]
        yt = [a3[:, 8 + 2 * n:10 + 2 * n, 0:HALF] for n in range(4)]
        hflat = hT[:, :, :, :].rearrange("p a k s -> p (a k s)")

        def a_slot(a, width, phase):
            if phase == "mix":
                both = ws[:, 3, a, :]
            else:
                both = hflat[:, a * 1024:(a + 1) * 1024]
            return both[:, 0:width], both[:, 512:512 + width]

        x_landed = [sem(f"x_landed{n}") for n in range(NT)]
        gpre_landed = sem("gpre_landed")
        const_landed = sem("const_landed")
        rel_landed = sem("rel_landed")
        ext_stored = sem("ext_stored")
        bias_landed = sem("bias_landed")
        ext_ready = sem("ext_ready")
        consts_made = sem("consts_made")
        bias_turned = sem("bias_turned")
        bias_ready = sem("bias_ready")
        raw_landed = [sem(f"raw_landed{n}") for n in range(2)]
        w_hi = sem("w_hi")
        w_split = sem("w_split")
        chunk_used = sem("chunk_used")
        x_sq = sem("x_sq")
        h_ready = sem("h_ready")
        hT_psum = sem("hT_psum")
        hT_hi = sem("hT_hi")
        hT_done = sem("hT_done")
        proj_free = sem("proj_free")
        vT_psum = sem("vT_psum")
        v_ready = sem("v_ready")
        qk_ready = sem("qk_ready")
        scores_psum = sem("scores_psum")
        biased = sem("biased")
        exp_done = sem("exp_done")
        pT_psum = sem("pT_psum")
        pT_act = sem("pT_act")
        pT_dve = sem("pT_dve")
        o_psum = sem("o_psum")
        o_sq = sem("o_sq")
        o_ready = sem("o_ready")
        unit_free = sem("unit_free")
        conv_sq = sem("conv_sq")
        conv_rs = sem("conv_rs")
        mix_done = sem("mix_done")
        gmix_landed = sem("gmix_landed")
        xr_landed = [sem(f"xr_landed{n}") for n in range(2)]
        a_hi = sem("a_hi")
        a_split = sem("a_split")
        y_psum = sem("y_psum")
        y_copied = sem("y_copied")
        y_sq = sem("y_sq")
        x2_ready = sem("x2_ready")
        x2_sq = sem("x2_sq")
        x2_stored = [sem(f"x2_stored{n}") for n in range(2)]
        silu_done = sem("silu_done")
        act_done = sem("act_done")
        gffn_landed = sem("gffn_landed")
        x2_landed = [sem(f"x2_landed{n}") for n in range(4)]
        f_psum = sem("f_psum")
        f_copied = sem("f_copied")
        f_sq = sem("f_sq")
        out_ready = sem("out_ready")
        out_stored = [sem(f"out_stored{n}") for n in range(4)]
        dve_seq = sem("dve_seq")

        block = ctx.enter_context(nc.Block())

        def keys(u):
            i = u // 2
            first = max(0, i - LEFT // P)
            return first, (i - first + 1) * P

        @block.sync
        def _(sp):
            def load(slot, src):
                sp.dma_start(raw[:, slot, :].rearrange("p (k n) -> p k n", k=KT) if len(src.shape) == 3
                             else raw[:, slot, :], src).then_inc(raw_landed[slot], 16)

            def free(g):
                sp.wait_ge(w_split, g - 1)

            def col(w, at):
                return w[:, :, bass.ds(at, P)]

            o_hc, o_bg, o_cg, o_q, o_k, o_v = [CONV * n for n in range(6)]
            sp.dma_start(row(0), x_d[0:P, :]).then_inc(x_landed[0], 16)
            sp.dma_start(row(GPRE), g_pre_mix[0].partition_broadcast(P)).then_inc(gpre_landed, 16)
            for n in range(1, NT):
                sp.dma_start(row(n), x_d[n * P:(n + 1) * P, :]).then_inc(x_landed[n], 16)
                if n == 4:
                    load(0, win_d[:, :, o_q:o_q + P])
                if n == 6:
                    load(1, win_d[:, :, o_k:o_k + P])
            free(2)
            load(0, win_d[:, :, o_v:o_v + P])
            with sp.Fori(0, PAIRS - 1) as t:
                for f, at in enumerate((o_hc, o_cg, o_bg, o_q + P, o_k + P, o_v + P)):
                    free(t * 6 + 3 + f)
                    load((3 + f) % 2, col(win_d, t * P + at))
            for f, at in enumerate((o_hc, o_cg, o_bg)):
                free(OUT0 - 3 + f)
                load((OUT0 - 3 + f) % 2, win_d[:, :, at + (PAIRS - 1) * P:at + PAIRS * P])
            for g in range(OUT0, FIN0):
                m = (g - OUT0) % KT
                free(g)
                load(g % 2, wout_d[m * P:(m + 1) * P, :])
            with sp.Fori(0, NF) as j:
                for gu in range(2):
                    free(j * 2 + FIN0 + gu)
                    load(gu, col(fin_d, j * P + gu * FF))
            for hf in range(2):
                with sp.Fori(0, NF // 2) as ff:
                    for c in range(2):
                        free(ff * 2 + FOUT0 + hf * NF + c)
                        load(c, fout_d[bass.ds(ff * 2 * P + c * P, P), :])

        @block.gpsimd
        def _(pool):
            pool.dma_start(relb[:, :], rel_bias[0]).then_inc(rel_landed, 16)
            with nc.allow_non_contiguous_dma("a few small parameters"):
                pool.dma_start(params[:, :, 0:TAPS], w_conv[0].rearrange("(t p) k -> p t k", p=P)
                               ).then_inc(const_landed, 16)
                pool.dma_start(params[:, :, 3:4], g_conv_out[0].rearrange("(t p o) -> p t o", p=P, o=1)
                               ).then_inc(const_landed, 16)
                pool.dma_start(params[:, :, 4:5], g_attn_out[0].rearrange("(t p o) -> p t o", p=P, o=1)
                               ).then_inc(const_landed, 16)
            nc.gpsimd.memset(ident[:, :], 0.0).then_inc(consts_made, 1)
            pool.wait_ge(consts_made, 1)
            nc.gpsimd.affine_select(out=ident[:, :], in_=ident[:, :], compare_op=ALU.not_equal, fill=1.0,
                                    base=0, pattern=[[-1, P]], channel_multiplier=1).then_inc(consts_made, 1)
            pool.wait_ge(consts_made, 2)
            nc.gpsimd.memset(group[:, :], 0.0).then_inc(consts_made, 1)
            pool.wait_ge(consts_made, 3)
            nc.gpsimd.memset(group[0:HD, 0:1], 1.0).then_inc(consts_made, 1)
            pool.wait_ge(consts_made, 4)
            nc.gpsimd.memset(group[HD:P, 1:2], 1.0).then_inc(consts_made, 1)
            pool.wait_ge(consts_made, 5)
            pool.wait_ge(rel_landed, 16)
            near = P - 1 + CLIP
            nc.gpsimd.tensor_copy(ext[:, near:ERW], relb[:, REL - 1:REL].broadcast_to([HEADS, ERW - near])
                                  ).then_inc(ext_ready, 1)
            pool.wait_ge(ext_ready, 1)
            nc.gpsimd.tensor_copy(ext[:, 0:near], relb[:, CLIP + 1 - P:REL - 1]).then_inc(ext_ready, 1)
            pool.wait_ge(ext_ready, 2)
            pool.dma_start(ext_d, ext).then_inc(ext_stored, 16)
            pool.wait_ge(ext_stored, 16)
            for n in range(2):
                turned = misc[:, :].rearrange("p (h b) -> p h b", b=BAND)
                pool.dma_start(turned, bass.AP(ext_d.tensor, 4 * n * ERW, [[1, P], [ERW, 4], [1, BAND]])
                               ).then_inc(bias_landed, 16)
                pool.wait_ge(bias_landed, 16 * n + 16)
                for h in range(4):
                    nc.gpsimd.tensor_copy(bias[:, (4 * n + h) * BAND:(4 * n + h + 1) * BAND],
                                          turned[:, h, ::-1]).then_inc(bias_turned, 1)
                    pool.wait_ge(bias_turned, 4 * n + h + 1)
            b3 = bias.rearrange("p (h b) -> p h b", h=HEADS)
            nc.gpsimd.memset(b3[0:CHUNK, :, BAND - CHUNK:BAND], NEG).then_inc(bias_ready, 1)
            pool.wait_ge(bias_ready, 1)
            nc.gpsimd.memset(b3[CHUNK:P, :, 0:CHUNK], NEG).then_inc(bias_ready, 1)

            pool.wait_ge(mix_done, 1)
            pool.dma_start(row(GPM), g_post_mix[0].partition_broadcast(P)).then_inc(gmix_landed, 16)
            pool.dma_start(row(GPF), g_pre_ffn[0].partition_broadcast(P)).then_inc(gmix_landed, 16)
            for i in range(NT):
                if i >= 2:
                    pool.wait_ge(h_ready, NT + i - 1)
                    pool.wait_ge(x2_stored[i % 2], 16 * (i // 2))
                pool.dma_start(row(XS[i % 2]), x_d[i * P:(i + 1) * P, :]).then_inc(xr_landed[i % 2], 16)
                if i >= 1:
                    pool.wait_ge(x2_ready, i)
                    pool.dma_start(x2_d[(i - 1) * P:i * P, :], row(XS[(i - 1) % 2])
                                   ).then_inc(x2_stored[(i - 1) % 2], 16)
            pool.wait_ge(x2_ready, NT)
            pool.dma_start(x2_d[(NT - 1) * P:NT * P, :], row(XS[(NT - 1) % 2])
                           ).then_inc(x2_stored[(NT - 1) % 2], 16)

            pool.wait_ge(act_done, NF + 2)
            pool.dma_start(sil[0], g_post_ffn[0].partition_broadcast(P)).then_inc(gffn_landed, 16)
            for n in range(2):
                pool.wait_ge(x2_stored[n], 16 * (NT // 2))
            for hf in range(2):
                for n in range(4):
                    i = 4 * hf + n
                    if hf == 0:
                        pool.wait_ge(a_split, OUT0 + NF)
                    else:
                        pool.wait_ge(out_ready, i - 3)
                    pool.dma_start(x2t[n], x2_d[i * P:(i + 1) * P, :].rearrange("p (a b) -> p a b", a=2)
                                   ).then_inc(x2_landed[n], 16)
                for n in range(4):
                    i = 4 * hf + n
                    pool.wait_ge(out_ready, i + 1)
                    pool.dma_start(out_d[i * P:(i + 1) * P, :].rearrange("p (a b) -> p a b", a=2), yt[n]
                                   ).then_inc(out_stored[n], 16)
            for n in range(4):
                pool.wait_ge(out_stored[n], 32)

        @block.tensor
        def _(pe):
            mm = nc.tensor.matmul
            tr = nc.tensor.transpose

            def transpose_h(n, src, pair, wait_pair):
                pe.wait_ge(h_ready, n + 1)
                if wait_pair:
                    wait_pair()
                for k in range(KT):
                    last = tr(PP[pair][:, k * P:(k + 1) * P], row(src)[:, k * P:(k + 1) * P], ident[:, :])
                last.then_inc(hT_psum, 1)

            def project(slot, k, pair):
                w = [ws[:, slot, part, k * P:(k + 1) * P] for part in range(2)]
                for wp, hp in ((0, 0), (0, 1), (1, 0)):
                    for half in range(2):
                        last = mm(PP[pair][:, half * HALF:(half + 1) * HALF], w[wp],
                                  hT[:, hp, k, half * HALF:(half + 1) * HALF],
                                  start=(k == 0 and (wp, hp) == (0, 0)), stop=(k == KT - 1 and wp == 1))
                if k == KT - 1:
                    last.then_inc(chunk_used, 1)

            def scores(u):
                h, (first, n) = u % 2, keys(u)
                pair = PP[u % 3]
                for at in range(0, n, 512):
                    w = min(512, n - at)
                    last = mm(pair[:, at:at + w], row(Q, P, (u // 2) * P)[h * HD:(h + 1) * HD, :],
                              row(K, w, first * P + at)[h * HD:(h + 1) * HD, :], start=True, stop=True)
                last.then_inc(scores_psum, 1)

            def transpose_p(u):
                _, n = keys(u)
                for j in range(n // P):
                    last = tr(PP[u % 3][:, j * P:(j + 1) * P], s_sb[u % 2][:, j * P:(j + 1) * P], ident[:, :])
                last.then_inc(pT_psum, 1)

            def times_v(u):
                h, (first, n) = u % 2, keys(u)
                for j in range(n // P):
                    last = mm(PP[u % 3][:, 640:640 + HD], pT[u % 2][:, j * P:(j + 1) * P],
                              row(V, HD, (first + j) * P + h * HD), start=(j == 0), stop=(j == n // P - 1))
                last.then_inc(o_psum, 1)

            def attend(t, groups, conv_at):
                pe.wait_ge(qk_ready, t * 2 + 2)
                for s in range(STEPS):
                    mine = list(groups[s])

                    def fill(n):
                        for _ in range(min(n, len(mine))):
                            f, k = mine.pop(0)
                            if k == 0:
                                pe.wait_ge(w_split, t * 6 + 4 + f)
                                pe.wait_ge(proj_free, t * 6 + 3 + f)
                            project((3 + f) % 2, k, 3)

                    if s < UNITS:
                        pe.wait_ge(unit_free, t * (STEPS - 2) + 1 + max(0, s - 2))
                        if s == 2:
                            pe.wait_ge(v_ready, t * 2 + 2)
                        scores(s)
                    if s != UNITS + 1:
                        fill(1)
                    if s == 0:
                        pe.wait_ge(proj_free, t * 6 + 3)
                        for i in range(NT):
                            last = tr(PP[2][:, i * P:(i + 1) * P], row(VN, P, i * P), ident[:, :])
                        last.then_inc(vT_psum, 1)
                    if 1 <= s <= UNITS:
                        pe.wait_ge(exp_done, t * UNITS + s)
                        transpose_p(s - 1)
                    if s != UNITS + 1:
                        fill(1)
                    if 2 <= s <= UNITS + 1:
                        pe.wait_ge(pT_act, t * UNITS + s - 1)
                        if s - 2 >= 8:
                            pe.wait_ge(pT_dve, t * 8 + s - 9)
                    bank = PP[(s - 2) % 3]
                    if s >= 3 and s % 2 == 0:
                        i = (s - 4) // 2
                        pe.wait_ge(o_ready, t * NT + i + 1)
                        last = tr(bank[:, 768:768 + P], o_raw[:, i % 2, :], ident[:, :])
                        if s == STEPS - 1:
                            last.then_inc(o_psum, 1)
                    if s == conv_at:
                        pe.wait_ge(conv_sq, t + 1)
                        for i in range(NT):
                            mm(bank[:, 2 * i:2 * i + 2], row(CU, P, i * P), group[:, :], start=True, stop=True)
                    if s in (conv_at + 2, conv_at + 3):
                        pe.wait_ge(conv_rs, t + 1)
                        for b in range(4):
                            i = 4 * (s - conv_at - 2) + b
                            tr(bank[:, b * P:(b + 1) * P], row(CR, P, i * P), ident[:, :])
                    if 2 <= s <= UNITS + 1:
                        times_v(s - 2)
                    fill(8)

            pe.wait_ge(consts_made, 5)
            for n in range(NT):
                transpose_h(n, H_A[n % 2], n % 2, (lambda n=n: pe.wait_ge(hT_done, n - 1)) if n >= 2 else None)
            pe.wait_ge(hT_done, NT)
            for f, pair in enumerate((3, 2, 3)):
                pe.wait_ge(w_split, f + 1)
                if f == 2:
                    pe.wait_ge(proj_free, 1)
                for k in range(KT):
                    project(f % 2, k, pair)
            full = [[(s // 3, k) for k in range(8) if k // 3 == s % 3] for s in range(18)] + [[]]
            late = [[(s // 4, 2 * (s % 4) + k) for k in range(2)] if s < 12 else [] for s in range(19)]
            with pe.Fori(0, PAIRS - 1) as t:
                attend(t, full, 10)
            attend(PAIRS - 1, late, 13)

            def out_pair(i):
                return i % 4 if i < 6 else i - 4

            def down(c, slot, a, tiles, pairs, width, phase, first, last_k, done):
                hi, lo = a_slot(a, width, phase)
                for n, _ in enumerate(tiles):
                    pair = PP[pairs[n]]
                    if first:
                        first(n)
                    for ap, wp in ((hi, 0), (hi, 1), (lo, 0)):
                        for half in range(2):
                            last = mm(pair[:, half * 512:(half + 1) * 512], ap[:, n * P:(n + 1) * P],
                                      ws[:, slot, wp, half * 512:(half + 1) * 512],
                                      start=(first is not None and ap is hi and wp == 0),
                                      stop=(last_k and ap is lo))
                    if last_k and n < len(tiles) - 1:
                        last.then_inc(done, 1)
                last.then_inc(chunk_used, 1)

            def h_pair(i):
                return {0: 2, 1: 2, 2: 2, 3: 0, 4: 0, 5: 0, 6: 0, 7: 1}[i]

            def o_transpose(i):
                def wait_pair():
                    pe.wait_ge(y_copied, {0: 3, 1: 3, 2: 3, 3: 6, 4: 6, 5: 6, 6: 6, 7: 6}[i])
                    if i not in (0, 3, 7):
                        pe.wait_ge(hT_done, NT + i)
                transpose_h(NT + i, H_O[i % 2], h_pair(i), wait_pair)

            pe.wait_ge(unit_free, PAIRS * (STEPS - 2) + 1)
            for p, tiles in enumerate(PASSES):
                pairs = [out_pair(i) for i in tiles]
                for m in range(KT):
                    c = p * KT + m
                    pe.wait_ge(w_split, OUT0 + c + 1)
                    pe.wait_ge(a_split, c + 1)

                    def begin(n, p=p, tiles=tiles):
                        if p == 1 and n >= 1:
                            pe.wait_ge(y_copied, n)
                        if p == 2:
                            pe.wait_ge(hT_done if n == 0 else y_copied, NT + 3 if n == 0 else 4)
                    if p and m in (3, 5, 7):
                        o_transpose(PASSES[p - 1][(m - 3) // 2])
                    down(c, c % 3, c % 2, tiles, pairs, len(tiles) * P, "mix", begin if m == 0 else None,
                         m == KT - 1, y_psum)
            for i in PASSES[2]:
                o_transpose(i)

            pe.wait_ge(hT_done, 2 * NT)
            with pe.Fori(0, NF // 2) as jj:
                for par in range(2):
                    pe.wait_ge(act_done, jj * 2 + par + 1)
                    for gu in range(2):
                        pe.wait_ge(w_split, jj * 4 + FIN0 + 2 * par + gu + 1)
                        for k in range(KT):
                            project(2 * par + gu, k, 2 * par + gu)

            def ffn_out(g, slot, hf, first, last_k):
                pe.wait_ge(w_split, g + 1)
                pe.wait_ge(a_split, g - FOUT0 + OUT0 + 1)

                def begin(n):
                    if hf == 0:
                        pe.wait_ge(act_done, NF + (1 if n < 2 else 2))
                    else:
                        pe.wait_ge(f_copied, n + 1)
                down(None, slot, slot, range(4), range(4), 512, "ffn", begin if first else None, last_k, f_psum)

            ffn_out(FOUT0, 0, 0, True, False)
            for c in (1, 2, 3):
                ffn_out(FOUT0 + c, c, 0, False, False)
            with pe.Fori(0, 4) as r:
                for c in range(4):
                    ffn_out(r * 4 + FOUT0 + 4 + c, c, 0, False, False)
            ffn_out(FOUT0 + 20, 0, 0, False, False)
            ffn_out(FOUT0 + 21, 1, 0, False, True)
            ffn_out(FOUT0 + 22, 2, 1, True, False)
            for c in range(3, 6):
                ffn_out(FOUT0 + 20 + c, c % 4, 1, False, False)
            with pe.Fori(0, 3) as r:
                for c in range(4):
                    ffn_out(r * 4 + FOUT0 + 26 + c, (c + 2) % 4, 1, False, False)
            for c in range(38, 44):
                ffn_out(FOUT0 + c, c % 4, 1, False, c == 43)

        @block.scalar
        def _(act):
            go = nc.scalar.activation

            def high(g, slot, raw_slot, wait_used):
                act.wait_ge(raw_landed[raw_slot], (g // 2) * 16 + 16 if isinstance(g, int) else g)
                if wait_used is not None:
                    act.wait_ge(chunk_used, wait_used)
                go(ws[:, slot, 0, :], raw[:, raw_slot, :], ACT.Copy).then_inc(w_hi, 1)

            def high_r(landed, slot, raw_slot, wait_used):
                act.wait_ge(raw_landed[raw_slot], landed)
                act.wait_ge(chunk_used, wait_used)
                go(ws[:, slot, 0, :], raw[:, raw_slot, :], ACT.Copy).then_inc(w_hi, 1)

            last_junk = []

            def square(src, dst, acc, done):
                if last_junk:
                    act.wait_ge(*last_junk[-1])
                go(dst, src, ACT.Square, accum_out=acc).then_inc(done[0], 1)
                last_junk.append(done)

            def high_hT(n, pair):
                act.wait_ge(hT_psum, n + 1)
                i = n % NT
                go(hT[:, 0, :, i * P:(i + 1) * P], PP[pair][:, :].rearrange("p (k s) -> p k s", s=P),
                   ACT.Copy).then_inc(hT_hi, 1)

            def sq_x(n):
                act.wait_ge(x_landed[n], 16)
                square(row(n), row(JUNK), ssq[:, n:n + 1], (x_sq, n + 1))

            for n in range(NT):
                sq_x(n)
                if n >= 2:
                    high_hT(n - 2, n % 2)
                if n == 6:
                    high(0, 0, 0, None)
            high_hT(6, 0)
            high(1, 1, 1, None)
            high_hT(7, 1)
            scale = HD ** -0.5
            high(2, 0, 0, 1)
            act.wait_ge(chunk_used, 1)
            go(row(Q), PP[3][:, :], ACT.Copy, scale=scale).then_inc(proj_free, 1)
            high(3, 1, 1, 2)
            act.wait_ge(proj_free, 2)
            act.wait_ge(chunk_used, 3)
            go(row(VN), PP[3][:, :], ACT.Copy).then_inc(proj_free, 1)

            def attend(t, evac, splits, conv_at):
                for s in range(STEPS):
                    if s in evac:
                        f = evac[s]
                        dst = {0: CV, 3: QN, 4: KN, 5: VN}[f]
                        act.wait_ge(chunk_used, t * 6 + 4 + f)
                        go(row(dst), PP[3][:, :], ACT.Copy).then_inc(proj_free, 1)
                    if s < UNITS:
                        act.wait_ge(biased, t * UNITS + s + 1)
                        _, n = keys(s)
                        go(s_sb[s % 2][:, 0:n], s_sb[s % 2][:, 0:n], ACT.Exp, bias=nmax[:, s % 2:s % 2 + 1],
                           accum_out=lsum[:, s % 4:s % 4 + 1]).then_inc(exp_done, 1)
                    if s == 0:
                        act.wait_ge(vT_psum, t + 1)
                        go(row(V, 512), PP[2][:, 0:512], ACT.Copy).then_inc(v_ready, 1)
                    if 1 <= s <= UNITS:
                        u = s - 1
                        _, n = keys(u)
                        act.wait_ge(pT_psum, t * UNITS + u + 1)
                        if u >= 2:
                            act.wait_ge(o_psum, t * (UNITS + 1) + u - 1)
                        go(pT[u % 2][:, 0:min(n, 512)], PP[u % 3][:, 0:min(n, 512)], ACT.Copy).then_inc(pT_act, 1)
                    if 2 <= s <= UNITS + 1:
                        u = s - 2
                        act.wait_ge(unit_free, t * (STEPS - 2) + u + 2)
                        o = o_raw[:, (u // 2) % 2, (u % 2) * HD:(u % 2 + 1) * HD]
                        if s > 2:
                            act.wait_ge(o_sq, t * UNITS + u)
                        go(sq_junk[:, :], o, ACT.Square, scale=HD ** -0.5, accum_out=osq[:, u % 2:u % 2 + 1]
                           ).then_inc(o_sq, 1)
                    if s == conv_at - 1:
                        act.wait_ge(proj_free, t * 6 + 3 + 3)
                        go(row(CU), row(CV), ACT.Square).then_inc(conv_sq, 1)
                    if s in splits:
                        f = splits[s]
                        g = 3 + f
                        high_r((t * 3 + g // 2) * 16 + 16, f_slot(f), g % 2, t * 6 + g - 1)
                    if s == UNITS and evac is full_evac:
                        act.wait_ge(scores_psum, t * UNITS + UNITS)
                        act.wait_ge(proj_free, t * 6 + 3 + 4)
                        go(row(Q), row(QN), ACT.Copy, scale=scale).then_inc(qk_ready, 1)
                if evac is full_evac:
                    act.wait_ge(chunk_used, t * 6 + 9)
                    go(row(VN), PP[3][:, :], ACT.Copy).then_inc(proj_free, 1)

            full_evac = {3: 0, 12: 3, 15: 4}

            def f_slot(f):
                return (3 + f) % 2

            with act.Fori(0, PAIRS - 1) as t:
                attend(t, full_evac, {1: 1, 4: 2, 7: 3, 10: 4, 13: 5, 16: 6}, 10)
            attend(PAIRS - 1, {4: 0}, {1: 1, 5: 2}, 13)

            def split_out(c):
                g = OUT0 + c
                tiles = PASSES[c // KT]
                width = len(tiles) * P
                act.wait_ge(raw_landed[g % 2], (g // 2) * 16 + 16)
                act.wait_ge(chunk_used, g - 2 if c >= 3 else (g - 1 if c < 2 else g - 2))
                go(ws[:, c % 3, 0, :], raw[:, g % 2, :], ACT.Copy).then_inc(w_hi, 1)
                if c >= 2:
                    act.wait_ge(chunk_used, g - 1)
                hi, _ = a_slot(c % 2, width, "mix")
                if c == 0:
                    act.wait_ge(mix_done, 1)
                go(hi, row(yT + c % KT, width, tiles[0] * P), ACT.Copy).then_inc(a_hi, 1)

            def copy_y(i):
                act.wait_ge(y_psum_of(i), y_value(i))
                if i >= 3:
                    act.wait_ge(x2_ready, i - 2)
                go(row(YS[i % 3]), PP[out_pair(i)][:, :], ACT.Copy).then_inc(y_copied, 1)

            def sq_y(i):
                act.wait_ge(y_copied, i + 1)
                square(row(YS[i % 3]), row(JUNK), ssq[:, 8 + i:9 + i], (y_sq, i + 1))

            def sq_x2(i):
                act.wait_ge(x2_ready, i + 1)
                square(row(XS[i % 2]), row(JUNK), ssq[:, 16 + i:17 + i], (x2_sq, i + 1))

            def out_pair(i):
                return i % 4 if i < 6 else i - 4

            def h_pair(i):
                return {0: 2, 1: 2, 2: 2, 3: 0, 4: 0, 5: 0, 6: 0, 7: 1}[i]

            def y_psum_of(i):
                return chunk_used if i in (2, 5, 7) else y_psum

            def y_value(i):
                return {0: 1, 1: 2, 2: OUT0 + 8, 3: 3, 4: 4, 5: OUT0 + 16, 6: 5, 7: OUT0 + 24}[i]

            split_out(0)
            for c in range(len(PASSES) * KT):
                if c + 1 < len(PASSES) * KT:
                    split_out(c + 1)
                p, m = c // KT, c % KT
                if p:
                    a, b, d = PASSES[p - 1]
                    if m == 0:
                        copy_y(a), copy_y(b), copy_y(d), sq_y(a)
                    if m == 1:
                        sq_y(b)
                    if m == 2:
                        sq_x2(a), sq_y(d)
                    if m == 3:
                        sq_x2(b), high_hT(NT + a, h_pair(a))
                    if m == 5:
                        sq_x2(d), high_hT(NT + b, h_pair(b))
                    if m == 7:
                        high_hT(NT + d, h_pair(d))
            a, b = PASSES[2]
            copy_y(a), copy_y(b), sq_y(a), sq_y(b)
            high(FIN0, 0, 0, FIN0 - 2)
            high(FIN0 + 1, 1, 1, FIN0 - 1)
            sq_x2(a), high_hT(NT + a, h_pair(a)), sq_x2(b), high_hT(NT + b, h_pair(b))

            with act.Fori(0, NF // 2) as jj:
                for par in range(2):
                    for gu in range(2):
                        landed = (jj * 2 + FIN0 // 2 + par + 1) * 16 + 16
                        high_r(landed, (2 * par + 2 + gu) % 4, gu, jj * 4 + FIN0 + 2 * par + gu)
                        if gu == 0:
                            act.wait_ge(act_done, jj * 2 + par + 1)
                            act.wait_ge(chunk_used, jj * 4 + FIN0 + 2 * par + 1)
                            go(sil[par], PP[2 * par][:, :], ACT.Silu).then_inc(silu_done, 1)

            def ffn_high(g, landed, slot, hf, f, with_w=True):
                act.wait_ge(chunk_used, g - 3)
                hi, _ = a_slot(slot, 512, "ffn")
                go(hi, arena[:, bass.ds(f * SEQ + hf * HALF, HALF)], ACT.Copy).then_inc(a_hi, 1)
                if with_w:
                    high_r(landed, (slot + 2) % 4, slot % 2, g - 1)

            def half_done(hf):
                for n in range(4):
                    i = 4 * hf + n
                    if n < 3:
                        act.wait_ge(f_psum, 3 * hf + n + 1)
                    else:
                        act.wait_ge(chunk_used, FOUT0 + NF * (hf + 1))
                    if hf:
                        act.wait_ge(out_stored[n], 16)
                    go(yt[n], PP[n][:, :].rearrange("p (a b) -> p a b", a=2), ACT.Copy).then_inc(f_copied, 1)
                for n in range(4):
                    i = 4 * hf + n
                    act.wait_ge(f_copied, i + 1)
                    square(yt[n], sil[1].rearrange("p (a b) -> p a b", a=2), ssq[:, 24 + i:25 + i],
                           (f_sq, i + 1))

            def landed_of(c):
                return ((FOUT0 + 2 + c) // 2) * 16 + 16

            act.wait_ge(chunk_used, FOUT0)
            act.wait_ge(act_done, NF + 2)
            with act.Fori(0, 5) as r:
                for c in range(4):
                    ffn_high(r * 4 + FOUT0 + c, r * 32 + landed_of(c), c, 0, r * 4 + c)
            for c in range(20, 24):
                ffn_high(FOUT0 + c, landed_of(c), c % 4, c // NF, c % NF)
            half_done(0)
            for c in range(24, 28):
                ffn_high(FOUT0 + c, landed_of(c), c % 4, 1, c - NF)
            with act.Fori(0, 3) as r:
                for c in range(28, 32):
                    ffn_high(r * 4 + FOUT0 + c, r * 32 + landed_of(c), c % 4, 1, r * 4 + c - NF)
            for c in range(40, 44):
                ffn_high(FOUT0 + c, landed_of(c), c % 4, 1, c - NF, c < 42)
            half_done(1)

        @block.vector
        def _(dve):
            chain = Chain(dve, dve_seq)
            ts, tt, stt = nc.vector.tensor_scalar, nc.vector.tensor_tensor, nc.vector.scalar_tensor_tensor

            def rsqrt(dst, v, n):
                y, a = dst, newt[:, 0:n]
                chain(ts(y.bitcast(I32), v.bitcast(I32), 1, None, ALU.logical_shift_right))
                chain(ts(y.bitcast(I32), y.bitcast(I32), -1, 0x5F3759DF, ALU.mult, ALU.add))
                for _ in range(3):
                    chain(tt(a, y, y, ALU.mult))
                    chain(stt(a, a, -0.5, v, ALU.mult, ALU.mult))
                    chain(stt(y, a, 1.5, y, ALU.add, ALU.mult))

            def low(n_hi, slot, raw_slot):
                dve.wait_ge(w_hi, n_hi)
                tt(ws[:, slot, 1, :], raw[:, raw_slot, :], ws[:, slot, 0, :].bitcast(F32),
                   ALU.subtract).then_inc(w_split, 1)

            def low_hT(n, pair, sem_=None):
                i = n % NT
                dve.wait_ge(hT_hi, n + 1)
                tt(hT[:, 1, :, i * P:(i + 1) * P], PP[pair][:, :].rearrange("p (k s) -> p k s", s=P),
                   hT[:, 0, :, i * P:(i + 1) * P].bitcast(F32), ALU.subtract).then_inc(hT_done, 1)

            dve.wait_ge(gpre_landed, 16)
            for n in range(0, NT, 2):
                dve.wait_ge(x_sq, n + 2)
                chain(ts(var[:, 0:2], ssq[:, n:n + 2], 1.0 / D, EPS, ALU.mult, ALU.add))
                rsqrt(rst[:, 0:2], var[:, 0:2], 2)
                for b in range(2):
                    i = n + b
                    if i >= 2:
                        dve.wait_ge(hT_psum, i - 1)
                    stt(row(H_A[i % 2]), row(i), rst[:, b:b + 1], row(GPRE), ALU.mult, ALU.mult
                        ).then_inc(h_ready, 1)
                    if i >= 2:
                        low_hT(i - 2, i % 2)
                if n == 6:
                    low(1, 0, 0)
            low_hT(6, 0)
            low(2, 1, 1)
            low_hT(7, 1)
            dve.wait_ge(hT_done, NT)
            dve.wait_ge(const_landed, 48)
            nc.vector.memset(cur[:, :], 0.0).then_inc(unit_free, 1)
            low(3, 0, 0)
            dve.wait_ge(proj_free, 1)
            dve.wait_ge(chunk_used, 2)
            nc.vector.tensor_copy(row(K), PP[2][:, :]).then_inc(proj_free, 1)
            low(4, 1, 1)
            dve.wait_ge(proj_free, 3)
            nc.vector.memset(nmax[:, :], 0.0).then_inc(qk_ready, 2)
            dve.wait_ge(bias_ready, 2)

            def attend(t, evac, taps_at, splits, conv_at, more):
                dve.wait_ge(unit_free, t * (STEPS - 2) + 1)
                chain(nc.vector.tensor_copy(cur[:, :], params[:, :, :].rearrange("p t c -> p (t c)")[
                    :, bass.ds(t * 5, 5)]))
                for s in range(STEPS):
                    if s in evac:
                        f = evac[s]
                        dve.wait_ge(chunk_used, t * 6 + 4 + f)
                        if f == 1:
                            nc.vector.memset(cu[:, 0:TAPS - 1], 0.0)
                            tt(cu[:, TAPS - 1:TAPS - 1 + SEQ], PP[3][:, :], row(CV), ALU.mult
                               ).then_inc(proj_free, 1)
                            dve.wait_ge(proj_free, t * 6 + 3 + 2)
                        else:
                            tt(row(CV), PP[3][:, :], row(CV), ALU.mult).then_inc(proj_free, 1)
                            dve.wait_ge(proj_free, t * 6 + 3 + 3)
                    if s < UNITS:
                        _, n = keys(s)
                        dve.wait_ge(scores_psum, t * UNITS + s + 1)
                        if s >= 2:
                            dve.wait_ge(pT_psum, t * UNITS + s - 1)
                        if s >= 1:
                            dve.wait_ge(biased, t * UNITS + s)
                        nc.vector.memset(gate[:, :], 0.0)
                        b = bias[:, (s % 2 + 1) * BAND - n:(s % 2 + 1) * BAND]
                        chain(nc.vector.tensor_tensor_reduce(
                            out=s_sb[s % 2][:, 0:n], in0=PP[s % 3][:, 0:n], in1=b, scale=1.0, scalar=-3e38,
                            op0=ALU.add, op1=ALU.max, accum_out=rst[:, 2:3]))
                        ts(nmax[:, s % 2:s % 2 + 1], rst[:, 2:3], -1.0, None, ALU.mult).then_inc(biased, 1)
                    if s == 0:
                        dve.wait_ge(vT_psum, t + 1)
                        nc.vector.tensor_copy(row(V, 512, 512), PP[2][:, 512:1024]).then_inc(v_ready, 1)
                    if 9 <= s <= UNITS:
                        u = s - 1
                        dve.wait_ge(pT_psum, t * UNITS + u + 1)
                        dve.wait_ge(o_psum, t * (UNITS + 1) + u - 1)
                        nc.vector.tensor_copy(pT[u % 2][:, 512:BAND], PP[u % 3][:, 512:BAND]).then_inc(pT_dve, 1)
                    bank = PP[(s - 2) % 3]
                    if s >= 2:
                        dve.wait_ge(o_psum, t * (UNITS + 1) + s - 1)
                        if s == conv_at:
                            chain(ts(var[:, :], bank[:, 0:16], 1.0 / HD, EPS, ALU.mult, ALU.add))
                        if s in (conv_at + 2, conv_at + 3):
                            at = 512 * (s - conv_at - 2)
                            stt(arena[:, bass.ds(t * SEQ + at, 512)], bank[:, 0:512], cur[:, 3:4],
                                row(CV, 512, at), ALU.mult, ALU.mult)
                        if s >= 3 and s % 2 == 0:
                            i = (s - 4) // 2
                            last = ts(arena[:, bass.ds((t + PAIRS) * SEQ + i * P, P)], bank[:, 768:768 + P],
                                      cur[:, 4:5], None, ALU.mult)
                        if s <= UNITS + 1:
                            u = s - 2
                            nc.vector.tensor_copy(o_raw[:, (u // 2) % 2, (u % 2) * HD:(u % 2 + 1) * HD],
                                                  bank[:, 640:640 + HD]).then_inc(unit_free, 1)
                        else:
                            last.then_inc(unit_free, 1)
                    if 3 <= s <= UNITS + 1 and s % 2 == 1:
                        i = (s - 3) // 2
                        ls = lsum[:, 2 * (i % 2):2 * (i % 2) + 2]
                        chain(stt(rst[:, 4:6], ls, EPS, ls, ALU.mult, ALU.mult))
                        dve.wait_ge(o_sq, t * UNITS + s - 1)
                        chain(tt(rst[:, 4:6], rst[:, 4:6], osq[:, :], ALU.add))
                        rsqrt(rst[:, 6:8], rst[:, 4:6], 2)
                        o3 = o_raw[:, i % 2, :].rearrange("p (h d) -> p h d", h=2)
                        tt(o3, o3, rst[:, 6:8].rearrange("p (h o) -> p h o", o=1).broadcast_to([P, 2, HD]),
                           ALU.mult).then_inc(o_ready, 1)
                    if taps_at <= s < taps_at + TAPS:
                        n = s - taps_at
                        if n == 0:
                            chain(ts(row(CV), cu[:, 0:SEQ], cur[:, 0:1], None, ALU.mult))
                        else:
                            chain(stt(row(CV), cu[:, n:n + SEQ], cur[:, n:n + 1], row(CV), ALU.mult, ALU.add))
                    if s == conv_at:
                        rsqrt(crs[:, :], var[:, :], 16)
                        nc.vector.tensor_copy(
                            row(CR).rearrange("p (g d) -> p g d", d=HD),
                            crs[:, :].rearrange("p (g o) -> p g o", o=1).broadcast_to([P, 16, HD])
                        ).then_inc(conv_rs, 1)
                    if s in splits:
                        f = splits[s]
                        g = 3 + f
                        low(t * 6 + g + 1, g % 2, g % 2)
                    if s == UNITS and more:
                        dve.wait_ge(scores_psum, t * UNITS + UNITS)
                        dve.wait_ge(proj_free, t * 6 + 3 + 5)
                        nc.vector.tensor_copy(row(K), row(KN)).then_inc(qk_ready, 1)
                        dve.wait_ge(biased, t * UNITS + UNITS)
                        chain(nc.vector.tensor_copy(bias[:, 0:2 * BAND],
                                                    bias[:, bass.ds((t + 1) * 2 * BAND, 2 * BAND)]))

            with dve.Fori(0, PAIRS - 1) as t, chain.loop(t, PAIRS - 1, 137):
                attend(t, {6: 1, 9: 2}, 6, {1: 1, 4: 2, 7: 3, 10: 4, 13: 5, 16: 6}, 10, True)
            attend(PAIRS - 1, {8: 1, 12: 2}, 8, {1: 1, 5: 2}, 13, False)
            dve.wait_ge(unit_free, PAIRS * (STEPS - 2) + 1)
            nc.vector.memset(newt[:, :], 0.0).then_inc(mix_done, 1)
            dve.wait_ge(mix_done, 1)

            def split_out(c):
                g = OUT0 + c
                tiles = PASSES[c // KT]
                width = len(tiles) * P
                low(g + 1, c % 3, g % 2)
                hi, lo = a_slot(c % 2, width, "mix")
                dve.wait_ge(a_hi, c + 1)
                tt(lo, row(yT + c % KT, width, tiles[0] * P), hi.bitcast(F32), ALU.subtract).then_inc(a_split, 1)

            def norm_y(i):
                dve.wait_ge(y_sq, i + 1)
                chain(ts(var[:, 0:1], ssq[:, 8 + i:9 + i], 1.0 / D, EPS, ALU.mult, ALU.add))
                rsqrt(rst[:, 0:1], var[:, 0:1], 1)
                y, xs = row(YS[i % 3]), row(XS[i % 2])
                chain(stt(y, y, rst[:, 0:1], row(GPM), ALU.mult, ALU.mult))
                dve.wait_ge(xr_landed[i % 2], 16 * (i // 2) + 16)
                tt(xs, y, xs, ALU.add).then_inc(x2_ready, 1)

            def norm_x2(i):
                dve.wait_ge(x2_sq, i + 1)
                chain(ts(var[:, 0:1], ssq[:, 16 + i:17 + i], 1.0 / D, EPS, ALU.mult, ALU.add))
                rsqrt(rst[:, 0:1], var[:, 0:1], 1)
                if i >= 2:
                    dve.wait_ge(hT_psum, NT + i - 1)
                stt(row(H_O[i % 2]), row(XS[i % 2]), rst[:, 0:1], row(GPF), ALU.mult, ALU.mult
                    ).then_inc(h_ready, 1)

            def h_pair(i):
                return {0: 2, 1: 2, 2: 2, 3: 0, 4: 0, 5: 0, 6: 0, 7: 1}[i]

            split_out(0)
            for c in range(len(PASSES) * KT):
                if c + 1 < len(PASSES) * KT:
                    split_out(c + 1)
                p, m = c // KT, c % KT
                if p:
                    a, b, d = PASSES[p - 1]
                    if c == KT:
                        dve.wait_ge(gmix_landed, 32)
                    if m == 1:
                        norm_y(a)
                    if m == 2:
                        norm_x2(a)
                    if m == 3:
                        norm_y(b), low_hT(NT + a, h_pair(a))
                    if m == 4:
                        norm_x2(b)
                    if m == 5:
                        norm_y(d), low_hT(NT + b, h_pair(b))
                    if m == 6:
                        norm_x2(d)
                    if m == 7:
                        low_hT(NT + d, h_pair(d))
            a, b = PASSES[2]
            norm_y(a), norm_y(b), norm_x2(a), norm_x2(b)
            low(FIN0 + 1, 0, 0)
            low(FIN0 + 2, 1, 1)
            low_hT(NT + a, h_pair(a)), low_hT(NT + b, h_pair(b))
            for n in range(2):
                dve.wait_ge(x2_stored[n], 16 * (NT // 2))
            dve.wait_ge(hT_done, 2 * NT)
            nc.vector.memset(newt[:, :], 0.0).then_inc(act_done, 2)

            with dve.Fori(0, NF // 2) as jj:
                for par in range(2):
                    for gu in range(2):
                        low(jj * 4 + FIN0 + 2 * par + gu + 3, (2 * par + 2 + gu) % 4, gu)
                    dve.wait_ge(silu_done, jj * 2 + par + 1)
                    dve.wait_ge(chunk_used, jj * 4 + FIN0 + 2 * par + 2)
                    tt(arena[:, bass.ds(jj * 2 * SEQ + par * SEQ, SEQ)], sil[par], PP[2 * par + 1][:, :],
                       ALU.mult).then_inc(act_done, 1)

            def ffn_low(g, slot, hf, f, with_w=True):
                hi, lo = a_slot(slot, 512, "ffn")
                dve.wait_ge(a_hi, g - FOUT0 + OUT0 + 1)
                tt(lo, arena[:, bass.ds(f * SEQ + hf * HALF, HALF)], hi.bitcast(F32), ALU.subtract
                   ).then_inc(a_split, 1)
                if with_w:
                    low(g + 3, (slot + 2) % 4, slot % 2)

            def half_done(hf):
                dve.wait_ge(gffn_landed, 16)
                for n in range(4):
                    i = 4 * hf + n
                    dve.wait_ge(f_sq, i + 1)
                    chain(ts(var[:, 0:1], ssq[:, 24 + i:25 + i], 1.0 / D, EPS, ALU.mult, ALU.add))
                    rsqrt(rst[:, 0:1], var[:, 0:1], 1)
                    g3 = sil[0].rearrange("p (a b) -> p a b", a=2)
                    chain(stt(yt[n], yt[n], rst[:, 0:1], g3, ALU.mult, ALU.mult))
                    dve.wait_ge(x2_landed[n], 16 * hf + 16)
                    tt(yt[n], yt[n], x2t[n], ALU.add).then_inc(out_ready, 1)

            dve.wait_ge(act_done, NF + 2)
            with dve.Fori(0, 5) as r:
                for c in range(4):
                    ffn_low(r * 4 + FOUT0 + c, c, 0, r * 4 + c)
            for c in range(20, 24):
                ffn_low(FOUT0 + c, c % 4, c // NF, c % NF)
            half_done(0)
            for c in range(24, 28):
                ffn_low(FOUT0 + c, c % 4, 1, c - NF)
            with dve.Fori(0, 3) as r:
                for c in range(28, 32):
                    ffn_low(r * 4 + FOUT0 + c, c % 4, 1, r * 4 + c - NF)
            for c in range(40, 44):
                ffn_low(FOUT0 + c, c % 4, 1, c - NF, c < 42)
            half_done(1)


_INS = ["x", "w_in", "w_conv", "rel_bias", "g_conv_out", "g_attn_out", "w_out", "g_pre_mix", "g_post_mix",
        "g_pre_ffn", "g_post_ffn", "w_ffn_in", "w_ffn_out"]


def kernel(**inputs):
    import numpy as np
    import concourse.bacc as bacc
    from concourse.bass_utils import run_bass_kernel_spmd

    nc = bacc.Bacc("TRN2", target_bir_lowering=False, num_devices=1)
    arrays, args = {}, []
    for name in _INS:
        a = np.ascontiguousarray(inputs[name])
        arrays[f"in_{name}"] = a
        args.append(nc.dram_tensor(f"in_{name}", a.shape, mybir.dt.from_np(a.dtype), kind="ExternalInput").ap())
    out = nc.dram_tensor("out_0", inputs["x"].shape, F32, kind="ExternalOutput").ap()
    trunk_layer(nc, *args, out)
    return run_bass_kernel_spmd(nc, [arrays], core_ids=[0]).results[0]["out_0"]
```

```python
from contextlib import ExitStack, contextmanager

import concourse.bass as bass
from concourse import mybir

F32 = mybir.dt.float32
F32R = mybir.dt.float32r
I32 = mybir.dt.int32
ALU = mybir.AluOpType
ACT = mybir.ActivationFunctionType

P = 128
EPS = 1e-6
NEG = -1e30


class Chain:

    def __init__(self, engine, sem):
        self.engine, self.sem, self.count, self.base = engine, sem, 0, 0

    def __call__(self, instruction):
        instruction.then_inc(self.sem, 1)
        self.count += 1
        self.engine.wait_ge(self.sem, self.base + self.count)

    @contextmanager
    def loop(self, i, rounds, per_round):
        before = self.count
        self.base = i * per_round
        yield
        assert self.count - before == per_round, (self.count - before, per_round)
        self.base = 0
        self.count = before + rounds * per_round


def trunk_layer(nc, x, w_in, w_conv, rel_bias, g_conv_out, g_attn_out, w_out, g_pre_mix, g_post_mix,
                g_pre_ffn, g_post_ffn, w_ffn_in, w_ffn_out, out):
    _, SEQ, D = x.shape
    _, CONV, TAPS = w_conv.shape
    _, HEADS, REL = rel_bias.shape
    ATTN = g_attn_out.shape[1]
    FF = w_ffn_out.shape[1]
    HD = ATTN // HEADS
    CLIP = (REL - 1) // 2
    CHUNK = 64
    LEFT = 8 * CHUNK

    NT = SEQ // P
    KT = D // P
    PAIRS = HEADS // 2
    UNITS = 2 * NT
    BAND = LEFT + P
    STEPS = UNITS + 2
    HALF = SEQ // 2
    NF = FF // P
    assert CONV // P == PAIRS and NT == 8 and KT == 8 and HD == 64 and D == SEQ == 1024 and NF == 22

    OUT0 = 6 * PAIRS
    PASSES = [(0, 1, 2), (3, 4, 5), (6, 7)]
    ROWS = [0, 1, 2, 4, 5, 6, 7, 3]
    FIN0 = OUT0 + len(PASSES) * KT
    FOUT0 = FIN0 + 2 * NF
    NOUT = len(PASSES) * KT

    x_d, out_d = x[0], out[0]
    win_d = w_in[0].rearrange("(k p) n -> p k n", p=P)
    wout_d = w_out[0]
    fin_d = w_ffn_in[0].rearrange("(k p) n -> p k n", p=P)
    fout_d = w_ffn_out[0]
    x2_d = nc.dram_tensor("x2_scratch", [SEQ, D], F32, kind="Internal").ap()
    ERW = BAND + P - 1
    ext_d = nc.dram_tensor("bias_scratch", [HEADS, ERW], F32, kind="Internal").ap()

    ctx = ExitStack()
    with ctx:
        def sb(name, shape, dt=F32):
            return ctx.enter_context(nc.sbuf_tensor(name, shape, dt))

        def sem(name):
            return ctx.enter_context(nc.semaphore(name))

        hT = sb("hT", [P, 2, KT, SEQ], F32R)
        ws = sb("ws", [P, 4, 2, D], F32R)
        raw = sb("raw", [P, 2, D])
        arena = sb("arena", [P, NF * SEQ])
        misc = sb("misc", [P, 4 * BAND])
        ident = sb("ident", [P, P])
        group = sb("group", [P, 2])
        params = sb("params", [P, PAIRS, 5])
        cur = sb("cur", [P, 5])
        nmax = sb("nmax", [P, 2])
        lsum = sb("lsum", [P, UNITS])
        osq = sb("osq", [P, UNITS])
        omax = sb("omax", [P, 1])
        o_raw = sb("o_raw", [P, NT, P])
        o_eps = sb("o_eps", [P, UNITS])
        ssq = sb("ssq", [P, 32])
        var = sb("var", [P, 16])
        rst = sb("rst", [P, 16])
        newt = sb("newt", [P, 16])
        crs = sb("crs", [P, 16])
        gate = sb("gate", [P, 1])
        sq_junk = sb("sq_junk", [P, HD])
        psum = ctx.enter_context(nc.psum_tensor("psum", [P, 4 * 1024], F32))
        PP = [psum[:, n * 1024:(n + 1) * 1024] for n in range(4)]

        def row(n, width=SEQ, at=0):
            return arena[:, n * SEQ + at:n * SEQ + at + width]

        yT = 0
        BIAS = 8
        QN, KN, VN, Q, K, V = 13, 14, 15, 16, 17, 18
        CV, CU, CR = 19, 20, 21
        cu = row(CU, SEQ + TAPS - 1)
        bias = arena[:, BIAS * SEQ:BIAS * SEQ + HEADS * BAND]
        s_sb = [misc[:, n * BAND:(n + 1) * BAND] for n in range(2)]
        pT = [misc[:, (2 + n) * BAND:(3 + n) * BAND] for n in range(2)]
        ext = row(CR, ERW)[0:HEADS, :]
        relb = row(CU, REL)[0:HEADS, :]
        JUNK = CV
        H_A = (QN, KN)
        GPRE = VN
        YS, XS, GPM, GPF, H_O = (8, 9, 10), (11, 12), 13, 14, (15, 16)
        sil = [misc[:, n * SEQ:(n + 1) * SEQ] for n in range(2)]
        a3 = arena[:, :].rearrange("p (f s) -> p f s", s=SEQ)
        x2t = [a3[:, 2 * n:2 * n + 2, 0:HALF] for n in range(4)]
        yt = [a3[:, 8 + 2 * n:10 + 2 * n, 0:HALF] for n in range(4)]
        hflat = hT[:, :, :, :].rearrange("p a k s -> p (a k s)")

        def banks_for_h(n):
            if n < NT:
                return (1024 * (n % 2) if n < 4 else 0), 512
            return {0: (2048, 512), 1: (2048, 512), 2: (2048, 512), 3: (0, 512), 4: (1024, 512),
                    5: (512, 1024), 6: (2560, 1024), 7: (512, 1024)}[n - NT]

        def h_psum(n, half):
            at, step = banks_for_h(n)
            return psum[:, at + half * step:at + half * step + 512]

        def h_parts(part, n):
            at, step = banks_for_h(n)
            to = hT[:, part, :, n % NT * P:(n % NT + 1) * P]
            if step == 512:
                return [(psum[:, at:at + 1024].rearrange("p (k s) -> p k s", s=P), to)]
            return [(h_psum(n, half).rearrange("p (k s) -> p k s", s=P), to[:, 4 * half:4 * half + 4, :])
                    for half in range(2)]

        def ffn_slot(g):
            return (2, 0, 1, 3)[g % 4]

        def a_slot(a, width, phase):
            if phase == "mix":
                both = ws[:, 3, a, :]
            else:
                both = hflat[:, a * 1024:(a + 1) * 1024]
            return both[:, 0:width], both[:, 512:512 + width]

        x_landed = [sem(f"x_landed{n}") for n in range(NT)]
        gpre_landed = sem("gpre_landed")
        const_landed = sem("const_landed")
        rel_landed = sem("rel_landed")
        ext_stored = sem("ext_stored")
        bias_landed = sem("bias_landed")
        ext_ready = sem("ext_ready")
        consts_made = sem("consts_made")
        bias_turned = sem("bias_turned")
        bias_ready = sem("bias_ready")
        raw_landed = [sem(f"raw_landed{n}") for n in range(2)]
        w_hi = sem("w_hi")
        w_split = sem("w_split")
        chunk_used = sem("chunk_used")
        x_sq = sem("x_sq")
        h_ready = sem("h_ready")
        hT_psum = sem("hT_psum")
        hT_hi = sem("hT_hi")
        hT_done = sem("hT_done")
        proj_free = sem("proj_free")
        vT_psum = sem("vT_psum")
        v_ready = sem("v_ready")
        qk_ready = sem("qk_ready")
        scores_psum = sem("scores_psum")
        biased = sem("biased")
        exp_done = sem("exp_done")
        pT_psum = sem("pT_psum")
        pT_act = sem("pT_act")
        pT_dve = sem("pT_dve")
        o_psum = sem("o_psum")
        o_sq = sem("o_sq")
        o_ready = sem("o_ready")
        unit_free = sem("unit_free")
        conv_sq = sem("conv_sq")
        conv_rs = sem("conv_rs")
        conv_stat = sem("conv_stat")
        conv_norm = sem("conv_norm")
        oT_psum = sem("oT_psum")
        oT_read = sem("oT_read")
        hT_free = sem("hT_free")
        mix_done = sem("mix_done")
        gmix_landed = sem("gmix_landed")
        xr_landed = [sem(f"xr_landed{n}") for n in range(2)]
        a_hi = sem("a_hi")
        a_split = sem("a_split")
        y_psum = sem("y_psum")
        y_copied = sem("y_copied")
        y_sq = sem("y_sq")
        x2_ready = sem("x2_ready")
        x2_sq = sem("x2_sq")
        x2_stored = [sem(f"x2_stored{n}") for n in range(2)]
        silu_done = sem("silu_done")
        act_done = sem("act_done")
        gffn_landed = sem("gffn_landed")
        x2_landed = [sem(f"x2_landed{n}") for n in range(4)]
        f_psum = sem("f_psum")
        f_copied = sem("f_copied")
        f_sq = sem("f_sq")
        out_ready = sem("out_ready")
        out_stored = [sem(f"out_stored{n}") for n in range(4)]
        dve_seq = sem("dve_seq")

        block = ctx.enter_context(nc.Block())

        def keys(u):
            i = u // 2
            first = max(0, i - LEFT // P)
            return first, (i - first + 1) * P

        @block.sync
        def _(sp):
            def load(slot, src):
                sp.dma_start(raw[:, slot, :].rearrange("p (k n) -> p k n", k=KT) if len(src.shape) == 3
                             else raw[:, slot, :], src).then_inc(raw_landed[slot], 16)

            def free(g):
                sp.wait_ge(w_split, g - 1)

            def col(w, at):
                return w[:, :, bass.ds(at, P)]

            o_hc, o_bg, o_cg, o_q, o_k, o_v = [CONV * n for n in range(6)]
            for n in range(NT):
                sp.dma_start(row(n), x_d[n * P:(n + 1) * P, :]).then_inc(x_landed[n], 16)
                if n == 1:
                    sp.dma_start(row(GPRE), g_pre_mix[0].partition_broadcast(P)).then_inc(gpre_landed, 16)
                if n == 3:
                    load(0, win_d[:, :, o_q:o_q + P])
                    load(1, win_d[:, :, o_k:o_k + P])
                if n == 5:
                    free(2)
                    load(0, win_d[:, :, o_v:o_v + P])
            with sp.Fori(0, PAIRS - 1) as t:
                for f, at in enumerate((o_hc, o_cg, o_bg, o_q + P, o_k + P, o_v + P)):
                    free(t * 6 + 3 + f)
                    load((3 + f) % 2, col(win_d, t * P + at))
            for f, at in enumerate((o_hc, o_cg, o_bg)):
                free(OUT0 - 3 + f)
                load((OUT0 - 3 + f) % 2, win_d[:, :, at + (PAIRS - 1) * P:at + PAIRS * P])
            for g in range(OUT0, FIN0):
                m = ROWS[(g - OUT0) % KT]
                free(g)
                load(g % 2, wout_d[m * P:(m + 1) * P, :])
            with sp.Fori(0, NF) as j:
                for gu in range(2):
                    free(j * 2 + FIN0 + gu)
                    load(gu, col(fin_d, j * P + gu * FF))
            for hf in range(2):
                with sp.Fori(0, NF // 2) as ff:
                    for c in range(2):
                        free(ff * 2 + FOUT0 + hf * NF + c)
                        load(c, fout_d[bass.ds(ff * 2 * P + c * P, P), :])

        @block.gpsimd
        def _(pool):
            pool.dma_start(relb, rel_bias[0]).then_inc(rel_landed, 16)
            with nc.allow_non_contiguous_dma("a few small parameters"):
                pool.dma_start(params[:, :, 0:TAPS], w_conv[0].rearrange("(t p) k -> p t k", p=P)
                               ).then_inc(const_landed, 16)
                pool.dma_start(params[:, :, 3:4], g_conv_out[0].rearrange("(t p o) -> p t o", p=P, o=1)
                               ).then_inc(const_landed, 16)
                pool.dma_start(params[:, :, 4:5], g_attn_out[0].rearrange("(t p o) -> p t o", p=P, o=1)
                               ).then_inc(const_landed, 16)
            nc.gpsimd.memset(ident[:, :], 0.0).then_inc(consts_made, 1)
            pool.wait_ge(consts_made, 1)
            nc.gpsimd.affine_select(out=ident[:, :], in_=ident[:, :], compare_op=ALU.not_equal, fill=1.0,
                                    base=0, pattern=[[-1, P]], channel_multiplier=1).then_inc(consts_made, 1)
            pool.wait_ge(consts_made, 2)
            nc.gpsimd.memset(group[:, :], 0.0).then_inc(consts_made, 1)
            pool.wait_ge(consts_made, 3)
            nc.gpsimd.memset(group[0:HD, 0:1], 1.0).then_inc(consts_made, 1)
            pool.wait_ge(consts_made, 4)
            nc.gpsimd.memset(group[HD:P, 1:2], 1.0).then_inc(consts_made, 1)
            pool.wait_ge(consts_made, 5)
            pool.wait_ge(rel_landed, 16)
            near = P - 1 + CLIP
            nc.gpsimd.tensor_copy(ext[:, near:ERW], relb[:, REL - 1:REL].broadcast_to([HEADS, ERW - near])
                                  ).then_inc(ext_ready, 1)
            pool.wait_ge(ext_ready, 1)
            nc.gpsimd.tensor_copy(ext[:, 0:near], relb[:, CLIP + 1 - P:REL - 1]).then_inc(ext_ready, 1)
            pool.wait_ge(ext_ready, 2)
            pool.dma_start(ext_d, ext).then_inc(ext_stored, 16)
            pool.wait_ge(ext_stored, 16)
            for n in range(2):
                turned = misc[:, :].rearrange("p (h b) -> p h b", b=BAND)
                pool.dma_start(turned, bass.AP(ext_d.tensor, 4 * n * ERW, [[1, P], [ERW, 4], [1, BAND]])
                               ).then_inc(bias_landed, 16)
                pool.wait_ge(bias_landed, 16 * n + 16)
                for h in range(4):
                    nc.gpsimd.tensor_copy(bias[:, (4 * n + h) * BAND:(4 * n + h + 1) * BAND],
                                          turned[:, h, ::-1]).then_inc(bias_turned, 1)
                    pool.wait_ge(bias_turned, 4 * n + h + 1)
            b3 = bias.rearrange("p (h b) -> p h b", h=HEADS)
            nc.gpsimd.memset(b3[0:CHUNK, :, BAND - CHUNK:BAND], NEG).then_inc(bias_ready, 1)
            pool.wait_ge(bias_ready, 1)
            nc.gpsimd.memset(b3[CHUNK:P, :, 0:CHUNK], NEG).then_inc(bias_ready, 1)

            pool.wait_ge(o_ready, PAIRS)
            pool.wait_ge(o_psum, PAIRS * UNITS)
            pool.dma_start(row(GPM), g_post_mix[0].partition_broadcast(P)).then_inc(gmix_landed, 16)
            pool.dma_start(row(GPF), g_pre_ffn[0].partition_broadcast(P)).then_inc(gmix_landed, 16)
            for i in range(NT):
                if i >= 2:
                    pool.wait_ge(h_ready, NT + i - 1)
                    pool.wait_ge(x2_stored[i % 2], 16 * (i // 2))
                pool.dma_start(row(XS[i % 2]), x_d[i * P:(i + 1) * P, :]).then_inc(xr_landed[i % 2], 16)
                if i >= 1:
                    pool.wait_ge(x2_ready, i)
                    pool.dma_start(x2_d[(i - 1) * P:i * P, :], row(XS[(i - 1) % 2])
                                   ).then_inc(x2_stored[(i - 1) % 2], 16)
            pool.wait_ge(x2_ready, NT)
            pool.dma_start(x2_d[(NT - 1) * P:NT * P, :], row(XS[(NT - 1) % 2])
                           ).then_inc(x2_stored[(NT - 1) % 2], 16)

            pool.wait_ge(act_done, NF)
            pool.dma_start(sil[0], g_post_ffn[0].partition_broadcast(P)).then_inc(gffn_landed, 16)
            for n in range(2):
                pool.wait_ge(x2_stored[n], 16 * (NT // 2))
            for hf in range(2):
                for n in range(4):
                    i = 4 * hf + n
                    if hf == 0:
                        pool.wait_ge(a_split, OUT0 + NF)
                    else:
                        pool.wait_ge(out_ready, i - 3)
                    pool.dma_start(x2t[n], x2_d[i * P:(i + 1) * P, :].rearrange("p (a b) -> p a b", a=2)
                                   ).then_inc(x2_landed[n], 16)
                for n in range(4):
                    i = 4 * hf + n
                    pool.wait_ge(out_ready, i + 1)
                    pool.dma_start(out_d[i * P:(i + 1) * P, :].rearrange("p (a b) -> p a b", a=2), yt[n]
                                   ).then_inc(out_stored[n], 16)
            for n in range(4):
                pool.wait_ge(out_stored[n], 32)

        @block.tensor
        def _(pe):
            mm = nc.tensor.matmul
            tr = nc.tensor.transpose

            def transpose_h(n, src):
                pe.wait_ge(h_ready, n + 1)
                for k in range(KT):
                    to = h_psum(n, k // 4)[:, k % 4 * P:(k % 4 + 1) * P]
                    last = tr(to, row(src)[:, k * P:(k + 1) * P], ident[:, :])
                last.then_inc(hT_psum, 1)

            def project(slot, k, pair, halves=(0, 1), signal=True):
                w = [ws[:, slot, part, k * P:(k + 1) * P] for part in range(2)]
                for wp, hp in ((0, 0), (0, 1), (1, 0)):
                    for half in halves:
                        last = mm(PP[pair][:, half * HALF:(half + 1) * HALF], w[wp],
                                  hT[:, hp, k, half * HALF:(half + 1) * HALF],
                                  start=(k == 0 and (wp, hp) == (0, 0)), stop=(k == KT - 1 and wp == 1))
                if k == KT - 1 and signal:
                    last.then_inc(chunk_used, 1)
                return last

            def scores(u):
                h, (first, n) = u % 2, keys(u)
                pair = PP[u % 3]
                for at in range(0, n, 512):
                    w = min(512, n - at)
                    last = mm(pair[:, at:at + w], row(Q, P, (u // 2) * P)[h * HD:(h + 1) * HD, :],
                              row(K, w, first * P + at)[h * HD:(h + 1) * HD, :], start=True, stop=True)
                last.then_inc(scores_psum, 1)

            def transpose_p(u):
                _, n = keys(u)
                for j in range(n // P):
                    last = tr(PP[u % 3][:, j * P:(j + 1) * P], s_sb[u % 2][:, j * P:(j + 1) * P], ident[:, :])
                last.then_inc(pT_psum, 1)

            def times_v(u):
                h, (first, n) = u % 2, keys(u)
                for j in range(n // P):
                    last = mm(PP[u % 3][:, 640:640 + HD], pT[u % 2][:, j * P:(j + 1) * P],
                              row(V, HD, (first + j) * P + h * HD), start=(j == 0), stop=(j == n // P - 1))
                last.then_inc(o_psum, 1)

            def step(t, s, groups, conv_at, post):
                mine = list(groups)

                def fill(n):
                    for _ in range(min(n, len(mine))):
                        f, k = mine.pop(0)
                        if k == 0:
                            pe.wait_ge(w_split, t * 6 + 4 + f)
                            pe.wait_ge(proj_free, t * 6 + 3 + f)
                        project((3 + f) % 2, k, 3)

                if s == 0:
                    pe.wait_ge(qk_ready, t * 2 + 2)
                if s < UNITS:
                    pe.wait_ge(unit_free, t * UNITS + 1 + max(0, s - 2))
                    if s == 2:
                        pe.wait_ge(v_ready, t * 2 + 2)
                    scores(s)
                fill(1)
                if s == 0:
                    pe.wait_ge(proj_free, t * 6 + 3)
                    for i in range(NT):
                        last = tr(PP[2][:, i * P:(i + 1) * P], row(VN, P, i * P), ident[:, :])
                    last.then_inc(vT_psum, 1)
                if 1 <= s <= UNITS:
                    pe.wait_ge(exp_done, t * UNITS + s)
                    transpose_p(s - 1)
                if post and s == 1:
                    pe.wait_ge(v_ready, t * 2 + 2)
                    transpose_o(t, 2)
                fill(1)
                if s >= 2:
                    pe.wait_ge(pT_act, t * UNITS + s - 1)
                    if s - 2 >= 8:
                        pe.wait_ge(pT_dve, t * 8 + s - 9)
                    bank = PP[(s - 2) % 3]
                    if s == conv_at:
                        pe.wait_ge(conv_sq, t + 1)
                        conv_stats(bank)
                    if conv_at and s in (conv_at + 2, conv_at + 3):
                        pe.wait_ge(conv_rs, t + 1)
                        conv_norms(bank, 4 * (s - conv_at - 2), 4)
                    times_v(s - 2)
                fill(8)
                if post and s == 1:
                    pe.wait_ge(oT_read, t)

            def transpose_o(t, pair):
                pe.wait_ge(o_ready, t)
                for i in range(NT):
                    last = tr(PP[pair][:, i * P:(i + 1) * P], row(CR, P, i * P), ident[:, :])
                last.then_inc(oT_psum, 1)

            def conv_stats(bank):
                for i in range(NT):
                    last = mm(bank[:, 2 * i:2 * i + 2], row(CU, P, i * P), group[:, :], start=True, stop=True)
                return last

            def conv_norms(bank, first, n):
                for b in range(n):
                    last = tr(bank[:, b * P:(b + 1) * P], row(CR, P, (first + b) * P), ident[:, :])
                return last

            def first_pair(f, half):
                if half == 0:
                    pe.wait_ge(w_split, f + 1)
                for k in range(KT):
                    project((2, 3, 0)[f], k, (3, 2, 1)[f], (half,), half == 1)

            def phase_a(n):
                if n >= 2:
                    pe.wait_ge(hT_done, n - 1 if n < 5 else n)
                transpose_h(n, H_A[n % 2])

            pe.wait_ge(consts_made, 5)
            for n in range(4):
                phase_a(n)
            pe.wait_ge(hT_done, 4)
            first_pair(0, 0)
            phase_a(4)
            phase_a(5)
            first_pair(1, 0)
            phase_a(6)
            phase_a(7)
            first_pair(2, 0)
            pe.wait_ge(hT_done, NT)
            for f in range(3):
                first_pair(f, 1)
            full = [[(s // 3, k) for k in range(8) if k // 3 == s % 3] for s in range(STEPS)]
            late = full[0:3] + [[(1, 0), (1, 1)]] + [[(1, k)] for k in range(2, 8)] + [[(2, k)] for k in range(8)]
            for s in range(2):
                step(0, s, full[s], None, False)
            with pe.Fori(0, PAIRS - 1) as t:
                for s in range(2, STEPS):
                    step(t, s, full[s], 10, False)
                for s in range(2):
                    step(t + 1, s, full[s], None, True)
            for s in range(2, STEPS):
                step(PAIRS - 1, s, late[s], None, False)

            def out_pair(i):
                return i % 4 if i < 6 else i - 4

            def down(slot, a, tiles, pairs, width, phase, first, last_k, done, signal=True):
                hi, lo = a_slot(a, width, phase)
                for n, tile in enumerate(tiles):
                    pair = PP[pairs[n]]
                    if first:
                        first(n)
                    for part, (ap, wp) in enumerate(((hi, 0), (hi, 1), (lo, 0))):
                        for half in range(2):
                            last = mm(pair[:, half * 512:(half + 1) * 512], ap[:, tile * P:(tile + 1) * P],
                                      ws[:, slot, wp, half * 512:(half + 1) * 512],
                                      start=(first is not None and part == 0), stop=(last_k and part == 2))
                    if last_k and n < len(tiles) - 1:
                        last.then_inc(done, 1)
                if signal:
                    last.then_inc(chunk_used, 1)
                return last

            pe.wait_ge(unit_free, PAIRS * UNITS + 1)
            before = {11: 0, 13: 1, 15: 2, 19: 3, 22: 4}
            for c in range(len(PASSES) * KT):
                p, m = c // KT, c % KT
                tiles = PASSES[p]
                if c in before:
                    i = before[c]
                    pe.wait_ge(y_copied, 3 if i < 3 else 6)
                    if i:
                        pe.wait_ge(hT_done, NT + i)
                    transpose_h(NT + i, H_O[i % 2])
                if c == 2:
                    pe.wait_ge(proj_free, OUT0)
                    transpose_o(PAIRS, 3)
                if c == 3:
                    pe.wait_ge(oT_read, PAIRS)
                    pe.wait_ge(conv_sq, PAIRS)
                    conv_stats(PP[3]).then_inc(conv_stat, 1)
                if c == 6:
                    pe.wait_ge(conv_rs, PAIRS)
                    conv_norms(PP[3], 0, NT).then_inc(conv_norm, 1)
                pe.wait_ge(w_split, OUT0 + c + 1)
                pe.wait_ge(a_split, c + 1)

                def begin(n, p=p):
                    if p == 1 and n == 0:
                        pe.wait_ge(mix_done, 1)
                    if p == 1 and n >= 1:
                        pe.wait_ge(y_copied, n)
                    if p == 2 and n == 0:
                        pe.wait_ge(hT_done, NT + 3)
                    if p == 2 and n == 1:
                        pe.wait_ge(y_copied, 4)
                down((c + 2) % 3, c % 2, range(len(tiles)), [out_pair(i) for i in tiles], len(tiles) * P, "mix",
                     begin if m == 0 else None, m == KT - 1, y_psum)

            def first_tiles(c, half):
                if half == 0:
                    pe.wait_ge(w_split, FIN0 + c + 1)
                for k in range(KT):
                    project(ffn_slot(c), k, c, (half,), half == 1)

            pe.wait_ge(hT_done, NT + 4)
            first_tiles(0, 0)
            pe.wait_ge(hT_done, NT + 5)
            transpose_h(NT + 5, H_O[1])
            first_tiles(1, 0)
            pe.wait_ge(y_copied, NT)
            first_tiles(2, 0)
            transpose_h(NT + 6, H_O[0])
            first_tiles(3, 0)
            pe.wait_ge(hT_done, NT + 6)
            transpose_h(NT + 7, H_O[1])
            pe.wait_ge(hT_done, 2 * NT)
            for c in range(4):
                first_tiles(c, 1)

            def ffn_in(j, par, last=False):
                pe.wait_ge(act_done, j - 1)
                for gu in range(2):
                    pe.wait_ge(w_split, j * 2 + FIN0 + gu + 1)
                    for k in range(KT):
                        done = project(ffn_slot(2 * par + gu), k, 2 * par + gu)
                        if last and gu == 1 and k < 4:
                            done.then_inc(hT_free, 1)

            with pe.Fori(1, NF // 2 - 1) as jj:
                for par in range(2):
                    ffn_in(jj * 2 + par, par)
            ffn_in(NF - 2, 0)
            ffn_in(NF - 1, 1, True)

            def ffn_out(g, c, hf, first, last_k):
                pe.wait_ge(w_split, g + 1)
                pe.wait_ge(a_split, g - FOUT0 + NOUT + 1)

                def begin(n):
                    if hf == 0:
                        pe.wait_ge(act_done, NF - 1 if n < 2 else NF)
                    else:
                        pe.wait_ge(f_copied, n + 1)
                down(ffn_slot(c), c % 4, range(4), range(4), 512, "ffn", begin if first else None, last_k, f_psum)

            for c in range(4):
                ffn_out(FOUT0 + c, c, 0, c == 0, False)
            with pe.Fori(1, 5) as r:
                for c in range(4):
                    ffn_out(r * 4 + FOUT0 + c, c, 0, False, False)
            for c in range(20, 28):
                hf = c // NF
                ffn_out(FOUT0 + c, c, hf, c % NF == 0, c % NF == NF - 1)
            with pe.Fori(0, 3) as r:
                for c in range(28, 32):
                    ffn_out(r * 4 + FOUT0 + c, c, 1, False, False)
            for n in range(4):
                for c in range(40, 44):
                    if n == 0:
                        pe.wait_ge(w_split, FOUT0 + c + 1)
                        pe.wait_ge(a_split, NOUT + c + 1)
                    last = down(ffn_slot(c), c % 4, (n,), (n,), 512, "ffn", None, c == 43, f_psum, False)
                last.then_inc(f_psum, 1)

        @block.scalar
        def _(act):
            go = nc.scalar.activation

            def high(g, slot, raw_slot, wait_used):
                act.wait_ge(raw_landed[raw_slot], (g // 2) * 16 + 16 if isinstance(g, int) else g)
                if wait_used is not None:
                    act.wait_ge(chunk_used, wait_used)
                go(ws[:, slot, 0, :], raw[:, raw_slot, :], ACT.Copy).then_inc(w_hi, 1)

            def high_r(landed, slot, raw_slot, wait_used):
                act.wait_ge(raw_landed[raw_slot], landed)
                act.wait_ge(chunk_used, wait_used)
                go(ws[:, slot, 0, :], raw[:, raw_slot, :], ACT.Copy).then_inc(w_hi, 1)

            last_junk = []

            def square(src, dst, acc, done):
                if last_junk:
                    act.wait_ge(*last_junk[-1])
                go(dst, src, ACT.Square, accum_out=acc).then_inc(done[0], 1)
                last_junk.append(done)

            def high_hT(n):
                act.wait_ge(hT_psum, n + 1)
                for src, dst in h_parts(0, n):
                    last = go(dst, src, ACT.Copy)
                last.then_inc(hT_hi, 1)

            def sq_x(n):
                act.wait_ge(x_landed[n], 16)
                square(row(n), row(JUNK), ssq[:, n:n + 1], (x_sq, n + 1))

            for n in range(4):
                sq_x(n)
            high_hT(0), high_hT(1), sq_x(4), high_hT(2), sq_x(5)
            high(0, 2, 0, None)
            high_hT(3), sq_x(6), sq_x(7)
            high(1, 3, 1, None)
            high_hT(4), high_hT(5)
            high(2, 0, 0, None)
            high_hT(6), high_hT(7)
            high(3, 1, 1, None)
            scale = HD ** -0.5
            act.wait_ge(chunk_used, 1)
            go(row(Q), PP[3], ACT.Copy, scale=scale).then_inc(proj_free, 1)
            act.wait_ge(proj_free, 2)
            act.wait_ge(chunk_used, 3)
            go(row(VN), PP[1], ACT.Copy).then_inc(proj_free, 1)

            def step(t, s, evac, splits, more, post):
                if s == 0 and post:
                    act.wait_ge(chunk_used, t * 6 + 3)
                    go(row(VN), PP[3], ACT.Copy).then_inc(proj_free, 1)
                if s in evac:
                    f = evac[s]
                    dst = {0: CV, 3: QN, 4: KN}[f]
                    act.wait_ge(chunk_used, t * 6 + 4 + f)
                    go(row(dst), PP[3], ACT.Copy).then_inc(proj_free, 1)
                if s < UNITS:
                    act.wait_ge(biased, t * UNITS + s + 1)
                    _, n = keys(s)
                    go(s_sb[s % 2][:, 0:n], s_sb[s % 2][:, 0:n], ACT.Exp, bias=nmax[:, s % 2:s % 2 + 1],
                       accum_out=lsum[:, s:s + 1]).then_inc(exp_done, 1)
                if s == 0:
                    act.wait_ge(vT_psum, t + 1)
                    go(row(V, 512), PP[2][:, 0:512], ACT.Copy).then_inc(v_ready, 1)
                if 1 <= s <= UNITS:
                    u = s - 1
                    _, n = keys(u)
                    act.wait_ge(pT_psum, t * UNITS + u + 1)
                    if u >= 2:
                        act.wait_ge(o_psum, t * UNITS + u - 1)
                    go(pT[u % 2][:, 0:min(n, 512)], PP[u % 3][:, 0:min(n, 512)], ACT.Copy).then_inc(pT_act, 1)
                if s in splits:
                    g = 3 + splits[s]
                    high_r((t * 3 + g // 2) * 16 + 16, g % 2, g % 2, t * 6 + g - 1)
                if s >= 2:
                    u = s - 2
                    act.wait_ge(unit_free, t * UNITS + u + 2)
                    if u:
                        act.wait_ge(o_sq, t * UNITS + u)
                    go(sq_junk[:, :], o_raw[:, u // 2, (u % 2) * HD:(u % 2 + 1) * HD], ACT.Square,
                       scale=HD ** -0.5, accum_out=osq[:, u:u + 1]).then_inc(o_sq, 1)
                if s == 9 and more:
                    square_conv(t)
                if s == UNITS and more:
                    act.wait_ge(scores_psum, t * UNITS + UNITS)
                    act.wait_ge(proj_free, t * 6 + 3 + 4)
                    go(row(Q), row(QN), ACT.Copy, scale=scale).then_inc(qk_ready, 1)

            def square_conv(t):
                act.wait_ge(proj_free, t * 6 + 3 + 3)
                go(row(CU), row(CV), ACT.Square).then_inc(conv_sq, 1)

            evac, splits = {3: 0, 12: 3, 15: 4}, {1: 1, 4: 2, 7: 3, 10: 4, 13: 5, 16: 6}
            for s in range(2):
                step(0, s, evac, splits, False, False)
            with act.Fori(0, PAIRS - 1) as t:
                for s in range(2, STEPS):
                    step(t, s, evac, splits, True, False)
                for s in range(2):
                    step(t + 1, s, evac, splits, False, True)

            def split_out(c):
                g = OUT0 + c
                tiles = PASSES[c // KT]
                width = len(tiles) * P
                act.wait_ge(raw_landed[g % 2], (g // 2) * 16 + 16)
                act.wait_ge(chunk_used, g - 2)
                go(ws[:, (c + 2) % 3, 0, :], raw[:, g % 2, :], ACT.Copy).then_inc(w_hi, 1)
                if c >= 2:
                    act.wait_ge(chunk_used, g - 1)
                if c == 6:
                    act.wait_ge(oT_read, PAIRS)
                if c == 7:
                    act.wait_ge(mix_done, 1)
                hi, _ = a_slot(c % 2, width, "mix")
                go(hi, row(yT + ROWS[c % KT], width, tiles[0] * P), ACT.Copy).then_inc(a_hi, 1)

            for s in range(2, STEPS):
                step(PAIRS - 1, s, {3: 0}, {4: 2}, False, False)
                if s == 6:
                    split_out(0)
                if s == 11:
                    split_out(1)
            square_conv(PAIRS - 1)

            def copy_y(i):
                done, value = {0: (y_psum, 1), 1: (y_psum, 2), 2: (chunk_used, OUT0 + KT),
                               3: (y_psum, 3), 4: (y_psum, 4), 5: (chunk_used, OUT0 + 2 * KT),
                               6: (y_psum, 5), 7: (chunk_used, OUT0 + 3 * KT)}[i]
                act.wait_ge(done, value)
                if i >= 3:
                    act.wait_ge(x2_ready, i - 2)
                pair = i % 4 if i < 6 else i - 4
                go(row(YS[i % 3]), PP[pair], ACT.Copy).then_inc(y_copied, 1)

            def sq_y(i):
                act.wait_ge(y_copied, i + 1)
                square(row(YS[i % 3]), row(JUNK), ssq[:, 8 + i:9 + i], (y_sq, i + 1))

            def sq_x2(i):
                act.wait_ge(x2_ready, i + 1)
                square(row(XS[i % 2]), row(JUNK), ssq[:, 16 + i:17 + i], (x2_sq, i + 1))

            tasks = {8: [(copy_y, 0), (copy_y, 1), (copy_y, 2), (sq_y, 0)], 9: [(sq_y, 1)],
                     10: [(sq_x2, 0), (sq_y, 2)], 11: [(high_hT, NT)], 12: [(sq_x2, 1)],
                     13: [(high_hT, NT + 1)], 14: [(sq_x2, 2)], 15: [(high_hT, NT + 2)],
                     16: [(copy_y, 3), (copy_y, 4), (copy_y, 5), (sq_y, 3)], 17: [(sq_y, 4)],
                     18: [(sq_x2, 3), (sq_y, 5)], 19: [(high_hT, NT + 3)], 21: [(sq_x2, 4)],
                     22: [(high_hT, NT + 4)]}
            for c in range(1, NOUT):
                if c + 1 < NOUT:
                    split_out(c + 1)
                for task, i in tasks.get(c, ()):
                    task(i)
            high(FIN0, ffn_slot(0), 0, FIN0 - 2)
            high(FIN0 + 1, ffn_slot(1), 1, FIN0 - 1)
            sq_x2(5), copy_y(6), copy_y(7), sq_y(6), high_hT(NT + 5), sq_y(7)
            high(FIN0 + 2, ffn_slot(2), 0, FIN0)
            sq_x2(6)
            high(FIN0 + 3, ffn_slot(3), 1, FIN0)
            high_hT(NT + 6), sq_x2(7), high_hT(NT + 7)

            def ffn_in(j, landed, par, more=True):
                act.wait_ge(chunk_used, j * 2 + FIN0 + 1)
                if not isinstance(j, int) or j >= 2:
                    act.wait_ge(act_done, j - 1)
                go(sil[par], PP[2 * par], ACT.Silu).then_inc(silu_done, 1)
                if more:
                    for gu in range(2):
                        high_r(landed, ffn_slot(2 * par + gu), gu, j * 2 + FIN0 + 1 + gu)

            for j in range(2):
                ffn_in(j, (FIN0 // 2 + j + 2) * 16 + 16, j)
            with act.Fori(1, NF // 2 - 1) as jj:
                for par in range(2):
                    ffn_in(jj * 2 + par, (jj * 2 + FIN0 // 2 + par + 2) * 16 + 16, par)
            ffn_in(NF - 2, (FIN0 // 2 + NF) * 16 + 16, 0)
            ffn_in(NF - 1, None, 1, False)

            def ffn_high(g, landed, c, hf, f, with_w=True):
                if isinstance(g, int) and g < FOUT0 + 4:
                    act.wait_ge(hT_free, c + 1)
                else:
                    act.wait_ge(chunk_used, g - 3)
                hi, _ = a_slot(c % 4, 512, "ffn")
                go(hi, arena[:, bass.ds(f * SEQ + hf * HALF, HALF)], ACT.Copy).then_inc(a_hi, 1)
                if with_w:
                    high_r(landed, ffn_slot(c + 2), c % 2, g - 1)

            def copy_f(n):
                act.wait_ge(*((f_psum, n + 1) if n < 3 else (chunk_used, FOUT0 + NF)))
                go(yt[n], PP[n].rearrange("p (a b) -> p a b", a=2), ACT.Copy).then_inc(f_copied, 1)

            def sq_f(i):
                if i < 4:
                    act.wait_ge(f_copied, i + 1)
                    square(yt[i], junk3, ssq[:, 24 + i:25 + i], (f_sq, i + 1))
                else:
                    act.wait_ge(f_psum, i)
                    square(PP[i - 4], sil[1], ssq[:, 24 + i:25 + i], (f_sq, i + 1))

            junk3 = sil[1].rearrange("p (a b) -> p a b", a=2)

            def landed_of(c):
                return ((FOUT0 + 2 + c) // 2) * 16 + 16

            for c in range(4):
                ffn_high(FOUT0 + c, landed_of(c), c, 0, c)
            with act.Fori(1, 5) as r:
                for c in range(4):
                    ffn_high(r * 4 + FOUT0 + c, r * 32 + landed_of(c), c, 0, r * 4 + c)
            for c in range(20, 28):
                if c == 24:
                    for n in range(4):
                        copy_f(n)
                ffn_high(FOUT0 + c, landed_of(c), c, c // NF, c % NF)
                if c >= 24:
                    sq_f(c - 24)
            with act.Fori(0, 3) as r:
                for c in range(28, 32):
                    ffn_high(r * 4 + FOUT0 + c, r * 32 + landed_of(c), c, 1, r * 4 + c - NF)
            for c in range(40, 44):
                ffn_high(FOUT0 + c, landed_of(c), c, 1, c - NF, c < 42)
            for i in range(4, NT):
                sq_f(i)

        @block.vector
        def _(dve):
            chain = Chain(dve, dve_seq)
            ts, tt, stt = nc.vector.tensor_scalar, nc.vector.tensor_tensor, nc.vector.scalar_tensor_tensor

            def rsqrt(dst, v, n):
                y, a = dst, newt[:, 0:n]
                chain(ts(y.bitcast(I32), v.bitcast(I32), 1, None, ALU.logical_shift_right))
                chain(ts(y.bitcast(I32), y.bitcast(I32), -1, 0x5F3759DF, ALU.mult, ALU.add))
                for _ in range(3):
                    chain(tt(a, y, y, ALU.mult))
                    chain(stt(a, a, -0.5, v, ALU.mult, ALU.mult))
                    chain(stt(y, a, 1.5, y, ALU.add, ALU.mult))

            def low(n_hi, slot, raw_slot):
                dve.wait_ge(w_hi, n_hi)
                tt(ws[:, slot, 1, :], raw[:, raw_slot, :], ws[:, slot, 0, :].bitcast(F32),
                   ALU.subtract).then_inc(w_split, 1)

            def low_hT(n):
                dve.wait_ge(hT_hi, n + 1)
                for (src, dst), (_, hi) in zip(h_parts(1, n), h_parts(0, n)):
                    last = tt(dst, src, hi.bitcast(F32), ALU.subtract)
                last.then_inc(hT_done, 1)

            dve.wait_ge(gpre_landed, 16)
            for n in range(0, NT, 2):
                dve.wait_ge(x_sq, n + 2)
                chain(ts(var[:, 0:2], ssq[:, n:n + 2], 1.0 / D, EPS, ALU.mult, ALU.add))
                rsqrt(rst[:, 0:2], var[:, 0:2], 2)
                for b in range(2):
                    i = n + b
                    if i >= 2:
                        dve.wait_ge(hT_psum, i - 1)
                    stt(row(H_A[i % 2]), row(i), rst[:, b:b + 1], row(GPRE), ALU.mult, ALU.mult
                        ).then_inc(h_ready, 1)
                    if i in (2, 3):
                        low_hT(i - 2)
                if n == 2:
                    low_hT(2), low(1, 2, 0), low_hT(3)
                if n == 4:
                    low(2, 3, 1), low_hT(4), low_hT(5)
            low(3, 0, 0)
            low_hT(6), low_hT(7)
            low(4, 1, 1)
            dve.wait_ge(hT_done, NT)
            dve.wait_ge(const_landed, 48)
            nc.vector.memset(gate[:, :], 0.0).then_inc(unit_free, 1)
            dve.wait_ge(proj_free, 1)
            dve.wait_ge(chunk_used, 2)
            nc.vector.tensor_copy(row(K), PP[2]).then_inc(proj_free, 1)
            dve.wait_ge(proj_free, 3)
            nc.vector.memset(nmax[:, :], 0.0).then_inc(qk_ready, 2)
            dve.wait_ge(bias_ready, 2)

            def step(t, s, evac, taps_at, splits, conv_at, more, post):
                if s == 0 and post:
                    chain(stt(o_eps[:, :], lsum[:, :], EPS, lsum[:, :], ALU.mult, ALU.mult))
                if s == 2:
                    chain(nc.vector.tensor_copy(cur[:, :], params[:, :, :].rearrange("p t c -> p (t c)")[
                        :, bass.ds(t * 5, 5)]))
                if s in evac:
                    f = evac[s]
                    dve.wait_ge(chunk_used, t * 6 + 4 + f)
                    if f == 1:
                        nc.vector.memset(cu[:, 0:TAPS - 1], 0.0)
                        tt(cu[:, TAPS - 1:TAPS - 1 + SEQ], PP[3], row(CV), ALU.mult).then_inc(proj_free, 1)
                        dve.wait_ge(proj_free, t * 6 + 3 + 2)
                    else:
                        conv_out(t)
                if s < UNITS:
                    _, n = keys(s)
                    dve.wait_ge(scores_psum, t * UNITS + s + 1)
                    if s >= 2:
                        dve.wait_ge(pT_psum, t * UNITS + s - 1)
                    if s >= 1:
                        dve.wait_ge(biased, t * UNITS + s)
                    nc.vector.memset(gate[:, :], 0.0)
                    b = bias[:, (s % 2 + 1) * BAND - n:(s % 2 + 1) * BAND]
                    chain(nc.vector.tensor_tensor_reduce(
                        out=s_sb[s % 2][:, 0:n], in0=PP[s % 3][:, 0:n], in1=b, scale=1.0, scalar=-3e38,
                        op0=ALU.add, op1=ALU.max, accum_out=omax[:, :]))
                    ts(nmax[:, s % 2:s % 2 + 1], omax[:, :], -1.0, None, ALU.mult).then_inc(biased, 1)
                if s == 0:
                    dve.wait_ge(vT_psum, t + 1)
                    nc.vector.tensor_copy(row(V, 512, 512), PP[2][:, 512:1024]).then_inc(v_ready, 1)
                if 9 <= s <= UNITS:
                    u = s - 1
                    dve.wait_ge(pT_psum, t * UNITS + u + 1)
                    dve.wait_ge(o_psum, t * UNITS + u - 1)
                    nc.vector.tensor_copy(pT[u % 2][:, 512:BAND], PP[u % 3][:, 512:BAND]).then_inc(pT_dve, 1)
                if s in splits:
                    g = 3 + splits[s]
                    low(t * 6 + g + 1, g % 2, g % 2)
                if s >= 2:
                    u = s - 2
                    bank = PP[u % 3]
                    dve.wait_ge(o_psum, t * UNITS + u + 1)
                    if s == conv_at:
                        chain(ts(var[:, :], bank[:, 0:16], 1.0 / HD, EPS, ALU.mult, ALU.add))
                    if conv_at and s in (conv_at + 2, conv_at + 3):
                        at = 512 * (s - conv_at - 2)
                        chain(stt(arena[:, bass.ds(t * SEQ + at, 512)], bank[:, 0:512], cur[:, 3:4],
                                  row(CV, 512, at), ALU.mult, ALU.mult))
                    nc.vector.tensor_copy(o_raw[:, u // 2, (u % 2) * HD:(u % 2 + 1) * HD],
                                          bank[:, 640:640 + HD]).then_inc(unit_free, 1)
                if s == 0 and post:
                    o_norm(t)
                if s == 1 and post:
                    o_scale(t)
                    o_finish(t, PP[2])
                if taps_at <= s < taps_at + TAPS:
                    n = s - taps_at
                    if n == 0:
                        chain(ts(row(CV), cu[:, 0:SEQ], cur[:, 0:1], None, ALU.mult))
                    else:
                        chain(stt(row(CV), cu[:, n:n + SEQ], cur[:, n:n + 1], row(CV), ALU.mult, ALU.add))
                if s == conv_at:
                    rsqrt(crs[:, :], var[:, :], 16)
                if conv_at and s == conv_at + 1:
                    conv_spread()
                if s == UNITS and more:
                    dve.wait_ge(scores_psum, t * UNITS + UNITS)
                    dve.wait_ge(proj_free, t * 6 + 3 + 5)
                    nc.vector.tensor_copy(row(K), row(KN)).then_inc(qk_ready, 1)
                    dve.wait_ge(biased, t * UNITS + UNITS)
                    chain(nc.vector.tensor_copy(bias[:, 0:2 * BAND],
                                                bias[:, bass.ds((t + 1) * 2 * BAND, 2 * BAND)]))

            def conv_out(t):
                tt(row(CV), PP[3], row(CV), ALU.mult).then_inc(proj_free, 1)
                dve.wait_ge(proj_free, t * 6 + 3 + 3)

            def conv_spread():
                nc.vector.tensor_copy(row(CR).rearrange("p (g d) -> p g d", d=HD),
                                      crs[:, :].rearrange("p (g o) -> p g o", o=1).broadcast_to([P, 16, HD])
                                      ).then_inc(conv_rs, 1)

            def o_norm(t):
                dve.wait_ge(o_sq, t * UNITS)
                chain(tt(o_eps[:, :], o_eps[:, :], osq[:, :], ALU.add))
                rsqrt(rst[:, :], o_eps[:, :], UNITS)

            def o_scale(t):
                tt(row(CR).rearrange("p (u d) -> p u d", d=HD),
                   o_raw[:, :, :].rearrange("p i (h d) -> p (i h) d", h=2),
                   rst[:, :].rearrange("p (u o) -> p u o", o=1).broadcast_to([P, UNITS, HD]),
                   ALU.mult).then_inc(o_ready, 1)
                dve.wait_ge(o_ready, t)

            def o_finish(t, pair):
                dve.wait_ge(oT_psum, t)
                ts(arena[:, bass.ds((t + PAIRS - 1) * SEQ, SEQ)], pair, cur[:, 4:5], None, ALU.mult
                   ).then_inc(oT_read, 1)
                dve.wait_ge(oT_read, t)

            args = ({6: 1, 9: 2}, 6, {1: 1, 4: 2, 7: 3, 10: 4, 13: 5, 16: 6}, 10)
            for s in range(2):
                step(0, s, *args, False, False)
            with dve.Fori(0, PAIRS - 1) as t, chain.loop(t, PAIRS - 1, 48):
                for s in range(2, STEPS):
                    step(t, s, *args, True, False)
                for s in range(2):
                    step(t + 1, s, *args, False, True)

            def split_out(c):
                g = OUT0 + c
                tiles = PASSES[c // KT]
                width = len(tiles) * P
                low(g + 1, (c + 2) % 3, g % 2)
                hi, lo = a_slot(c % 2, width, "mix")
                dve.wait_ge(a_hi, c + 1)
                tt(lo, row(yT + ROWS[c % KT], width, tiles[0] * P), hi.bitcast(F32), ALU.subtract
                   ).then_inc(a_split, 1)

            for s in range(2, STEPS):
                step(PAIRS - 1, s, {10: 1}, 10, {4: 2}, None, False, False)
                if s == 6:
                    split_out(0)
                if s == 11:
                    split_out(1)
            chain(stt(o_eps[:, :], lsum[:, :], EPS, lsum[:, :], ALU.mult, ALU.mult))
            dve.wait_ge(chunk_used, OUT0)
            conv_out(PAIRS - 1)
            o_norm(PAIRS)
            o_scale(PAIRS)

            def norm_y(i):
                dve.wait_ge(y_sq, i + 1)
                chain(ts(var[:, 0:1], ssq[:, 8 + i:9 + i], 1.0 / D, EPS, ALU.mult, ALU.add))
                rsqrt(rst[:, 0:1], var[:, 0:1], 1)
                y, xs = row(YS[i % 3]), row(XS[i % 2])
                chain(stt(y, y, rst[:, 0:1], row(GPM), ALU.mult, ALU.mult))
                dve.wait_ge(xr_landed[i % 2], 16 * (i // 2) + 16)
                tt(xs, y, xs, ALU.add).then_inc(x2_ready, 1)

            def norm_x2(i):
                dve.wait_ge(x2_sq, i + 1)
                chain(ts(var[:, 0:1], ssq[:, 16 + i:17 + i], 1.0 / D, EPS, ALU.mult, ALU.add))
                rsqrt(rst[:, 0:1], var[:, 0:1], 1)
                if i >= 2:
                    dve.wait_ge(hT_psum, NT + i - 1)
                stt(row(H_O[i % 2]), row(XS[i % 2]), rst[:, 0:1], row(GPF), ALU.mult, ALU.mult
                    ).then_inc(h_ready, 1)

            def conv_last_stats(_):
                dve.wait_ge(conv_stat, 1)
                chain(ts(var[:, :], PP[3][:, 0:16], 1.0 / HD, EPS, ALU.mult, ALU.add))
                rsqrt(crs[:, :], var[:, :], 16)
                dve.wait_ge(oT_psum, PAIRS)
                conv_spread()

            def conv_last(_):
                dve.wait_ge(conv_norm, 1)
                stt(row(PAIRS - 1), PP[3], cur[:, 3:4], row(CV), ALU.mult, ALU.mult).then_inc(mix_done, 1)
                dve.wait_ge(mix_done, 1)

            def attn_last(_):
                o_finish(PAIRS, PP[3])

            tasks = {1: [(attn_last, 0)], 3: [(conv_last_stats, 0)], 5: [(conv_last, 0)],
                     9: [(norm_y, 0)], 10: [(norm_x2, 0)], 11: [(norm_y, 1), (low_hT, NT)], 12: [(norm_x2, 1)],
                     13: [(norm_y, 2), (low_hT, NT + 1)], 14: [(norm_x2, 2)], 15: [(low_hT, NT + 2)],
                     17: [(norm_y, 3)], 18: [(norm_x2, 3)], 19: [(norm_y, 4), (low_hT, NT + 3)],
                     21: [(norm_x2, 4)], 22: [(low_hT, NT + 4), (norm_y, 5)]}
            for c in range(1, NOUT):
                if c + 1 < NOUT:
                    split_out(c + 1)
                if c == KT:
                    dve.wait_ge(gmix_landed, 32)
                for task, i in tasks.get(c, ()):
                    task(i)
            low(FIN0 + 1, ffn_slot(0), 0)
            norm_x2(5)
            low(FIN0 + 2, ffn_slot(1), 1)
            norm_y(6)
            low_hT(NT + 5)
            low(FIN0 + 3, ffn_slot(2), 0)
            norm_x2(6), norm_y(7)
            low(FIN0 + 4, ffn_slot(3), 1)
            low_hT(NT + 6), norm_x2(7), low_hT(NT + 7)
            for n in range(2):
                dve.wait_ge(x2_stored[n], 16 * (NT // 2))

            def ffn_in(j, par, more=True):
                if more:
                    low(j * 2 + FIN0 + 5, ffn_slot(2 * par), 0)
                dve.wait_ge(silu_done, j + 1)
                dve.wait_ge(chunk_used, j * 2 + FIN0 + 2)
                tt(arena[:, bass.ds(j * SEQ, SEQ)], sil[par], PP[2 * par + 1], ALU.mult).then_inc(act_done, 1)
                if more:
                    low(j * 2 + FIN0 + 6, ffn_slot(2 * par + 1), 1)

            for j in range(2):
                ffn_in(j, j)
            with dve.Fori(1, NF // 2 - 1) as jj:
                for par in range(2):
                    ffn_in(jj * 2 + par, par)
            ffn_in(NF - 2, 0)

            def ffn_low(g, c, hf, f, with_w=True):
                hi, lo = a_slot(c % 4, 512, "ffn")
                dve.wait_ge(a_hi, g - FOUT0 + NOUT + 1)
                tt(lo, arena[:, bass.ds(f * SEQ + hf * HALF, HALF)], hi.bitcast(F32), ALU.subtract
                   ).then_inc(a_split, 1)
                if with_w:
                    low(g + 3, ffn_slot(c + 2), c % 2)

            def norm_f(i):
                n, hf = i % 4, i // 4
                dve.wait_ge(f_sq, i + 1)
                chain(ts(var[:, 0:1], ssq[:, 24 + i:25 + i], 1.0 / D, EPS, ALU.mult, ALU.add))
                rsqrt(rst[:, 0:1], var[:, 0:1], 1)
                if hf:
                    dve.wait_ge(out_stored[n], 16)
                y = PP[n].rearrange("p (a b) -> p a b", a=2) if hf else yt[n]
                chain(stt(yt[n], y, rst[:, 0:1], sil[0].rearrange("p (a b) -> p a b", a=2), ALU.mult, ALU.mult))
                dve.wait_ge(x2_landed[n], 16 * hf + 16)
                tt(yt[n], yt[n], x2t[n], ALU.add).then_inc(out_ready, 1)

            dve.wait_ge(act_done, NF - 1)
            ffn_low(FOUT0, 0, 0, 0)
            ffn_low(FOUT0 + 1, 1, 0, 1, False)
            ffn_in(NF - 1, 1, False)
            low(FOUT0 + 4, ffn_slot(3), 1)
            dve.wait_ge(act_done, NF)
            for c in range(2, 4):
                ffn_low(FOUT0 + c, c, 0, c)
            with dve.Fori(1, 5) as r:
                for c in range(4):
                    ffn_low(r * 4 + FOUT0 + c, c, 0, r * 4 + c)
            for c in range(20, 28):
                ffn_low(FOUT0 + c, c, c // NF, c % NF)
                if c == 24:
                    dve.wait_ge(gffn_landed, 16)
                if c >= 24:
                    norm_f(c - 24)
            with dve.Fori(0, 3) as r:
                for c in range(28, 32):
                    ffn_low(r * 4 + FOUT0 + c, c, 1, r * 4 + c - NF)
            for c in range(40, 44):
                ffn_low(FOUT0 + c, c, 1, c - NF, c < 42)
            for i in range(4, NT):
                norm_f(i)


_INS = ["x", "w_in", "w_conv", "rel_bias", "g_conv_out", "g_attn_out", "w_out", "g_pre_mix", "g_post_mix",
        "g_pre_ffn", "g_post_ffn", "w_ffn_in", "w_ffn_out"]


def kernel(**inputs):
    import numpy as np
    import concourse.bacc as bacc
    from concourse.bass_utils import run_bass_kernel_spmd

    nc = bacc.Bacc("TRN2", target_bir_lowering=False, num_devices=1)
    arrays, args = {}, []
    for name in _INS:
        a = np.ascontiguousarray(inputs[name])
        arrays[f"in_{name}"] = a
        args.append(nc.dram_tensor(f"in_{name}", a.shape, mybir.dt.from_np(a.dtype), kind="ExternalInput").ap())
    out = nc.dram_tensor("out_0", inputs["x"].shape, F32, kind="ExternalOutput").ap()
    trunk_layer(nc, *args, out)
    return run_bass_kernel_spmd(nc, [arrays], core_ids=[0]).results[0]["out_0"]
```

```python
from contextlib import ExitStack, contextmanager

import concourse.bass as bass
from concourse import mybir

F32 = mybir.dt.float32
F32R = mybir.dt.float32r
I32 = mybir.dt.int32
ALU = mybir.AluOpType
ACT = mybir.ActivationFunctionType

P = 128
EPS = 1e-6
NEG = -1e30


class Chain:

    def __init__(self, engine, sem):
        self.engine, self.sem, self.count, self.base = engine, sem, 0, 0

    def __call__(self, instruction):
        instruction.then_inc(self.sem, 1)
        self.count += 1
        self.engine.wait_ge(self.sem, self.base + self.count)

    @contextmanager
    def loop(self, i, rounds, per_round):
        before = self.count
        self.base = i * per_round
        yield
        assert self.count - before == per_round, (self.count - before, per_round)
        self.base = 0
        self.count = before + rounds * per_round


def rsqrt_steps(engine, chain, y, v, a, b, last):
    tt, ts = engine.tensor_tensor, engine.tensor_scalar
    chain(ts(y.bitcast(I32), v.bitcast(I32), -0.5, float(0x5F3759DF), ALU.mult, ALU.add))
    chain(tt(a, y, y, ALU.mult))
    chain(tt(a, a, v, ALU.mult))
    chain(ts(a, a, -0.5, 1.5, ALU.mult, ALU.add))
    chain(tt(y, a, y, ALU.mult))
    chain(tt(a, y, y, ALU.mult))
    chain(tt(a, a, v, ALU.mult))
    chain(ts(b, a, 0.375, -1.25, ALU.mult, ALU.add))
    chain(tt(a, b, a, ALU.mult))
    chain(ts(a, a, 1.875, None, ALU.add))
    last(tt(y, a, y, ALU.mult))


def trunk_layer(nc, x, w_in, w_conv, rel_bias, g_conv_out, g_attn_out, w_out, g_pre_mix, g_post_mix,
                g_pre_ffn, g_post_ffn, w_ffn_in, w_ffn_out, out):
    _, SEQ, D = x.shape
    _, CONV, TAPS = w_conv.shape
    _, HEADS, REL = rel_bias.shape
    ATTN = g_attn_out.shape[1]
    FF = w_ffn_out.shape[1]
    HD = ATTN // HEADS
    CLIP = (REL - 1) // 2
    CHUNK = 64
    LEFT = 8 * CHUNK

    NT = SEQ // P
    KT = D // P
    PAIRS = HEADS // 2
    UNITS = 2 * NT
    BAND = LEFT + P
    STEPS = UNITS + 2
    HALF = SEQ // 2
    NF = FF // P
    assert CONV // P == PAIRS and NT == 8 and KT == 8 and HD == 64 and D == SEQ == 1024 and NF == 22

    OUT0 = 6 * PAIRS
    PASSES = [(0, 1, 2), (3, 4, 5), (6, 7)]
    ROWS = [0, 1, 2, 4, 5, 6, 7, 3] + [3, 7, 6, 0, 1, 2, 4, 5] + [5, 4, 2, 3, 7, 6, 0, 1]
    LOAD = list(range(8)) + [7, 6, 5] + list(range(8, 13)) + [12, 11, 10] + list(range(13, 18))
    AGAIN = 6
    FIN0 = OUT0 + max(LOAD) + 1
    FOUT0 = FIN0 + 2 * NF
    NOUT = len(PASSES) * KT

    x_d, out_d = x[0], out[0]
    win_d = w_in[0].rearrange("(k p) n -> p k n", p=P)
    wout_d = w_out[0]
    fin_d = w_ffn_in[0].rearrange("(k p) n -> p k n", p=P)
    fout_d = w_ffn_out[0]
    x2_d = nc.dram_tensor("x2_scratch", [SEQ, D], F32, kind="Internal").ap()
    ERW = BAND + P - 1
    ext_d = nc.dram_tensor("bias_scratch", [HEADS, ERW], F32, kind="Internal").ap()

    ctx = ExitStack()
    with ctx:
        def sb(name, shape, dt=F32):
            return ctx.enter_context(nc.sbuf_tensor(name, shape, dt))

        def sem(name):
            return ctx.enter_context(nc.semaphore(name))

        hT = sb("hT", [P, 2, KT, SEQ], F32R)
        ws = sb("ws", [P, 4, 2, D], F32R)
        raw = sb("raw", [P, 2, D])
        arena = sb("arena", [P, NF * SEQ])
        misc = sb("misc", [P, 4 * BAND])
        ident = sb("ident", [P, P])
        group = sb("group", [P, 2])
        params = sb("params", [P, PAIRS, 5])
        cur = sb("cur", [P, 5])
        nmax = sb("nmax", [P, 2])
        lsum = sb("lsum", [P, UNITS])
        osq = sb("osq", [P, UNITS])
        omax = sb("omax", [P, 1])
        o_raw = sb("o_raw", [P, NT, P])
        o_eps = sb("o_eps", [P, UNITS])
        ssq = sb("ssq", [P, 32])
        var = sb("var", [P, 16])
        rst = sb("rst", [P, 16])
        newt = sb("newt", [P, 16])
        newt_pool = sb("newt_pool", [P, 2, 16])
        var_pool = sb("var_pool", [P, 1])
        xrs = sb("xrs", [P, NT])
        yrs = sb("yrs", [P, NT])
        x2rs = sb("x2rs", [P, NT])
        crs = sb("crs", [P, 16])
        gate = sb("gate", [P, 1])
        sq_junk = sb("sq_junk", [P, HD])
        psum = ctx.enter_context(nc.psum_tensor("psum", [P, 4 * 1024], F32))
        PP = [psum[:, n * 1024:(n + 1) * 1024] for n in range(4)]

        def row(n, width=SEQ, at=0):
            return arena[:, n * SEQ + at:n * SEQ + at + width]

        yT = 0
        BIAS = 8
        QN, KN, VN, V = 13, 14, 15, 18
        CV, CU, CR = 19, 20, 21
        cu = row(CU, SEQ + TAPS - 1)
        q_parts, k_parts = [[ws[:, slot, part, :] for part in range(2)] for slot in (2, 3)]
        bias = arena[:, BIAS * SEQ:BIAS * SEQ + HEADS * BAND]
        s_sb = [misc[:, n * BAND:(n + 1) * BAND] for n in range(2)]
        pT = [misc[:, (2 + n) * BAND:(3 + n) * BAND] for n in range(2)]
        turned = misc[:, :].rearrange("p (h b) -> p h b", b=BAND)
        ext = row(CR, ERW)[0:HEADS, :]
        relb = row(CU, REL)[0:HEADS, :]
        JUNK = CV
        GPRE = VN
        YS, XS, GPM, GPF, H_O = (8, 9, 10), (11, 12, 17, 18), 13, 14, (15, 16)
        sil = [misc[:, n * SEQ:(n + 1) * SEQ] for n in range(2)]
        a3 = arena[:, :].rearrange("p (f s) -> p f s", s=SEQ)
        x2t = [a3[:, 2 * n:2 * n + 2, 0:HALF] for n in range(4)]
        yt = [a3[:, 8 + 2 * n:10 + 2 * n, 0:HALF] for n in range(4)]
        hflat = hT[:, :, :, :].rearrange("p a k s -> p (a k s)")

        def banks_for_h(n):
            if n < NT:
                return {5: (1536, 1024), 7: (2560, 1024)}.get(n, (1024 * (n % 3), 512) if n < 4 else (0, 512))
            return {0: (2048, 512), 1: (2048, 512), 2: (2048, 512), 3: (0, 512), 4: (1024, 512),
                    5: (512, 1024), 6: (2560, 1024), 7: (512, 1024)}[n - NT]

        def h_psum(n, half):
            at, step = banks_for_h(n)
            return psum[:, at + half * step:at + half * step + 512]

        def h_parts(part, n):
            at, step = banks_for_h(n)
            to = hT[:, part, :, n % NT * P:(n % NT + 1) * P]
            if step == 512:
                return [(psum[:, at:at + 1024].rearrange("p (k s) -> p k s", s=P), to)]
            return [(h_psum(n, half).rearrange("p (k s) -> p k s", s=P), to[:, 4 * half:4 * half + 4, :])
                    for half in range(2)]

        def split_ahead(c):
            if c < 2 * KT:
                return [c + 1]
            return [c + 1, c + 2] if c == 2 * KT else [c + 2] if c + 2 < NOUT else []

        def ffn_slot(g):
            return (1, 0, 2, 3)[g % 4]

        def out_slot(c):
            return ((0, 2, 1), (2, 0, 1), (0, 2, 1))[c // KT][c % KT % 3]

        def fresh(c):
            return LOAD[c] not in LOAD[:c]

        def mix_slot(c):
            return c % (4 if c // KT == 2 else 2)

        def a_slot(a, width, phase):
            if phase == "mix" and width <= 256:
                return tuple(ws[:, 3, a // 2, at:at + width] for at in (a % 2 * 512, a % 2 * 512 + 256))
            if phase == "mix":
                both = ws[:, 3, a, :]
            else:
                both = hflat[:, a * 1024:(a + 1) * 1024]
            return both[:, 0:width], both[:, 512:512 + width]

        x_landed = [sem(f"x_landed{n}") for n in range(NT)]
        gpre_landed = sem("gpre_landed")
        const_landed = sem("const_landed")
        rel_landed = sem("rel_landed")
        ext_stored = sem("ext_stored")
        bias_landed = sem("bias_landed")
        ext_ready = sem("ext_ready")
        consts_made = sem("consts_made")
        bias_turned = sem("bias_turned")
        bias_ready = sem("bias_ready")
        raw_landed = [sem(f"raw_landed{n}") for n in range(2)]
        w_hi = sem("w_hi")
        w_split = sem("w_split")
        chunk_used = sem("chunk_used")
        x_sq = sem("x_sq")
        x_rs = sem("x_rs")
        h_ready = sem("h_ready")
        hT_psum = sem("hT_psum")
        hT_hi = sem("hT_hi")
        hT_done = sem("hT_done")
        proj_free = sem("proj_free")
        vT_psum = sem("vT_psum")
        v_ready = sem("v_ready")
        qk_high = sem("qk_high")
        qk_ready = sem("qk_ready")
        scores_psum = sem("scores_psum")
        biased = sem("biased")
        exp_done = sem("exp_done")
        pT_psum = sem("pT_psum")
        pT_act = sem("pT_act")
        pT_dve = sem("pT_dve")
        o_psum = sem("o_psum")
        o_sq = sem("o_sq")
        o_ready = sem("o_ready")
        unit_free = sem("unit_free")
        conv_sq = sem("conv_sq")
        conv_factors = sem("conv_factors")
        conv_rs = sem("conv_rs")
        conv_stat = sem("conv_stat")
        conv_var = sem("conv_var")
        o_var = sem("o_var")
        o_rs = sem("o_rs")
        y_rs = sem("y_rs")
        x2_rs = sem("x2_rs")
        pool_seq = sem("pool_seq")
        conv_norm = sem("conv_norm")
        oT_psum = sem("oT_psum")
        oT_read = sem("oT_read")
        hT_free = sem("hT_free")
        mix_done = sem("mix_done")
        gmix_landed = sem("gmix_landed")
        xr_landed = [sem(f"xr_landed{n}") for n in range(4)]
        a_hi = sem("a_hi")
        a_split = sem("a_split")
        y_psum = sem("y_psum")
        y_copied = sem("y_copied")
        y_sq = sem("y_sq")
        x2_ready = sem("x2_ready")
        x2_sq = sem("x2_sq")
        x2_stored = [sem(f"x2_stored{n}") for n in range(4)]
        silu_done = sem("silu_done")
        act_done = sem("act_done")
        gffn_landed = sem("gffn_landed")
        x2_landed = [sem(f"x2_landed{n}") for n in range(4)]
        f_psum = sem("f_psum")
        f_copied = sem("f_copied")
        f_sq = sem("f_sq")
        out_ready = sem("out_ready")
        out_stored = [sem(f"out_stored{n}") for n in range(4)]
        last_stored = sem("last_stored")
        dve_seq = sem("dve_seq")

        block = ctx.enter_context(nc.Block())

        def keys(u):
            i = u // 2
            first = max(0, i - LEFT // P)
            return first, (i - first + 1) * P

        OUT_AT = 768

        def scores_at(u):
            return 128 if keys(u)[1] == BAND else 0

        CONV_AT = 13

        @block.sync
        def _(sp):
            def load(slot, src):
                sp.dma_start(raw[:, slot, :].rearrange("p (k n) -> p k n", k=KT) if len(src.shape) == 3
                             else raw[:, slot, :], src).then_inc(raw_landed[slot], 16)

            def free(g):
                sp.wait_ge(w_split, g - 1)

            def col(w, at):
                return w[:, :, bass.ds(at, P)]

            def load_x(i):
                sp.dma_start(row(XS[i % 4]), x_d[i * P:(i + 1) * P, :]).then_inc(xr_landed[i % 4], 16)

            X_AFTER = {12: 4, 13: 5, 14: 6, 17: 7}
            o_hc, o_bg, o_cg, o_q, o_k, o_v = [CONV * n for n in range(6)]
            for n in range(NT):
                sp.dma_start(row(n), x_d[n * P:(n + 1) * P, :]).then_inc(x_landed[n], 16)
                if n == 1:
                    sp.dma_start(row(GPRE), g_pre_mix[0].partition_broadcast(P)).then_inc(gpre_landed, 16)
                if n == 3:
                    load(0, win_d[:, :, o_q:o_q + P])
                if n == 5:
                    load(1, win_d[:, :, o_k:o_k + P])
            free(2)
            load(0, win_d[:, :, o_v:o_v + P])
            with sp.Fori(0, PAIRS - 1) as t:
                for f, at in enumerate((o_hc, o_cg, o_q + P, o_bg, o_k + P, o_v + P)):
                    free(t * 6 + 3 + f)
                    load((3 + f) % 2, col(win_d, t * P + at))
            for f, at in enumerate((o_hc, o_cg, o_bg)):
                free(OUT0 - 3 + f)
                load((OUT0 - 3 + f) % 2, win_d[:, :, at + (PAIRS - 1) * P:at + PAIRS * P])
            for g in range(OUT0, FIN0):
                m = ROWS[LOAD.index(g - OUT0)]
                free(g)
                load(g % 2, wout_d[m * P:(m + 1) * P, :])
                if g == OUT0 + 4:
                    sp.wait_ge(o_psum, PAIRS * UNITS)
                    sp.dma_start(row(GPM), g_post_mix[0].partition_broadcast(P)).then_inc(gmix_landed, 16)
                    sp.dma_start(row(GPF), g_pre_ffn[0].partition_broadcast(P)).then_inc(gmix_landed, 16)
                    for i in range(4):
                        load_x(i)
                if g - OUT0 in X_AFTER:
                    i = X_AFTER[g - OUT0]
                    sp.wait_ge(h_ready, NT + i - 3)
                    sp.wait_ge(x2_stored[i % 4], 16)
                    load_x(i)
            with sp.Fori(0, NF) as j:
                for gu in range(2):
                    free(j * 2 + FIN0 + gu)
                    load(gu, col(fin_d, j * P + gu * FF))
            for hf in range(2):
                with sp.Fori(0, NF // 2) as ff:
                    for c in range(2):
                        free(ff * 2 + FOUT0 + hf * NF + c)
                        load(c, fout_d[bass.ds(ff * 2 * P + c * P, P), :])
            for i in range(4, NT):
                sp.wait_ge(out_ready, i + 1)
                if i < NT - 1:
                    sp.dma_start(out_d[i * P:(i + 1) * P, :].rearrange("p (a b) -> p a b", a=2), yt[i - 4]
                                 ).then_inc(last_stored, 16)
            for part in range(2):
                sp.wait_ge(out_ready, NT + part)
                sp.dma_start(out_d[(NT - 1) * P:NT * P, part * HALF:(part + 1) * HALF], yt[3][:, part]
                             ).then_inc(last_stored, 16)
            sp.wait_ge(last_stored, 80)

        @block.gpsimd
        def _(pool):
            pool.dma_start(relb, rel_bias[0]).then_inc(rel_landed, 16)
            with nc.allow_non_contiguous_dma("a few small parameters"):
                pool.dma_start(params[:, :, 0:TAPS], w_conv[0].rearrange("(t p) k -> p t k", p=P)
                               ).then_inc(const_landed, 16)
                pool.dma_start(params[:, :, 3:4], g_conv_out[0].rearrange("(t p o) -> p t o", p=P, o=1)
                               ).then_inc(const_landed, 16)
                pool.dma_start(params[:, :, 4:5], g_attn_out[0].rearrange("(t p o) -> p t o", p=P, o=1)
                               ).then_inc(const_landed, 16)
            nc.gpsimd.memset(ident[:, :], 0.0).then_inc(consts_made, 1)
            pool.wait_ge(consts_made, 1)
            nc.gpsimd.affine_select(out=ident[:, :], in_=ident[:, :], compare_op=ALU.not_equal, fill=1.0,
                                    base=0, pattern=[[-1, P]], channel_multiplier=1).then_inc(consts_made, 1)
            pool.wait_ge(consts_made, 2)
            nc.gpsimd.memset(group[:, :], 0.0).then_inc(consts_made, 1)
            pool.wait_ge(consts_made, 3)
            nc.gpsimd.memset(group[0:HD, 0:1], 1.0).then_inc(consts_made, 1)
            pool.wait_ge(consts_made, 4)
            nc.gpsimd.memset(group[HD:P, 1:2], 1.0).then_inc(consts_made, 1)
            pool.wait_ge(consts_made, 5)
            pool.wait_ge(rel_landed, 16)
            near = P - 1 + CLIP
            nc.gpsimd.tensor_copy(ext[:, near:ERW], relb[:, REL - 1:REL].broadcast_to([HEADS, ERW - near])
                                  ).then_inc(ext_ready, 1)
            pool.wait_ge(ext_ready, 1)
            nc.gpsimd.tensor_copy(ext[:, 0:near], relb[:, CLIP + 1 - P:REL - 1]).then_inc(ext_ready, 1)
            pool.wait_ge(ext_ready, 2)
            pool.dma_start(ext_d, ext).then_inc(ext_stored, 16)
            chain = Chain(pool, pool_seq)

            def factors_to(y, v, n, done, value):
                rsqrt_steps(nc.gpsimd, chain, y, v, newt_pool[:, 0, 0:n], newt_pool[:, 1, 0:n],
                            lambda last: last.then_inc(done, 1))
                pool.wait_ge(done, value)

            def x_factors(first, end, value):
                pool.wait_ge(x_sq, end)
                v = crs[:, first:end]
                chain(nc.gpsimd.tensor_scalar(v, ssq[:, first:end], 1.0 / D, EPS, ALU.mult, ALU.add))
                factors_to(xrs[:, first:end], v, end - first, x_rs, value)

            x_factors(2, 4, 1)
            pool.wait_ge(ext_stored, 16)
            for n in range(2):
                pool.dma_start(turned, bass.AP(ext_d.tensor, 4 * n * ERW, [[1, P], [ERW, 4], [1, BAND]])
                               ).then_inc(bias_landed, 16)
                if n == 0:
                    x_factors(4, 6, 2)
                    x_factors(6, NT, 3)
                    pool.wait_ge(bias_landed, 16)
                    for h in range(4):
                        nc.gpsimd.tensor_copy(bias[:, h * BAND:(h + 1) * BAND], turned[:, h, ::-1]
                                              ).then_inc(bias_turned, 1)
                        pool.wait_ge(bias_turned, h + 1)
            pool.wait_ge(bias_turned, 8)
            b3 = bias.rearrange("p (h b) -> p h b", h=HEADS)
            nc.gpsimd.memset(b3[0:CHUNK, :, BAND - CHUNK:BAND], NEG).then_inc(bias_ready, 1)
            pool.wait_ge(bias_ready, 1)
            nc.gpsimd.memset(b3[CHUNK:P, :, 0:CHUNK], NEG).then_inc(bias_ready, 1)

            def conv_norm_factors(t):
                pool.wait_ge(conv_var, t + 1)
                factors_to(crs[:, :], var[:, :], 16, conv_factors, t + 1)

            def o_norm_factors(t):
                pool.wait_ge(o_var, t + 1)
                factors_to(rst[:, :], o_eps[:, :], UNITS, o_rs, t + 1)

            for t in range(PAIRS - 1):
                conv_norm_factors(t)
                o_norm_factors(t)
            o_norm_factors(PAIRS - 1)
            conv_norm_factors(PAIRS - 1)

            def norm_factor(i, sums, factors, done):
                chain(nc.gpsimd.tensor_scalar(var_pool[:, :], sums[:, i:i + 1], 1.0 / D, EPS, ALU.mult, ALU.add))
                factors_to(factors[:, i:i + 1], var_pool[:, :], 1, done, i + 1)

            def y_factor(i):
                pool.wait_ge(y_sq, i + 1)
                norm_factor(i, ssq[:, 8:16], yrs, y_rs)

            def x2_factor(i):
                pool.wait_ge(x2_sq, i + 1)
                norm_factor(i, ssq[:, 16:24], x2rs, x2_rs)

            y, x2 = y_factor, x2_factor
            for step, i in ((y, 0), (y, 1), (x2, 0), (y, 2), (x2, 1), (x2, 2), (y, 3), (y, 4), (x2, 3),
                            (y, 5), (x2, 4), (x2, 5), (y, 6), (y, 7), (x2, 6), (x2, 7)):
                step(i)

            pool.wait_ge(act_done, NF)
            pool.dma_start(sil[0], g_post_ffn[0].partition_broadcast(P)).then_inc(gffn_landed, 16)
            for n in range(4):
                pool.wait_ge(x2_stored[n], 16 * (NT // 4))
            for hf in range(2):
                for n in range(4):
                    i = 4 * hf + n
                    if hf == 0:
                        pool.wait_ge(a_split, NOUT + NF)
                    else:
                        pool.wait_ge(out_ready, i - 3)
                    pool.dma_start(x2t[n], x2_d[i * P:(i + 1) * P, :].rearrange("p (a b) -> p a b", a=2)
                                   ).then_inc(x2_landed[n], 16)
                for n in range(4 if hf == 0 else 0):
                    i = 4 * hf + n
                    pool.wait_ge(out_ready, i + 1)
                    pool.dma_start(out_d[i * P:(i + 1) * P, :].rearrange("p (a b) -> p a b", a=2), yt[n]
                                   ).then_inc(out_stored[n], 16)
            for n in range(4):
                pool.wait_ge(out_stored[n], 16)

        @block.tensor
        def _(pe):
            mm = nc.tensor.matmul
            tr = nc.tensor.transpose

            def transpose_h(n, src):
                pe.wait_ge(h_ready, n + 1)
                for k in range(KT):
                    to = h_psum(n, k // 4)[:, k % 4 * P:(k % 4 + 1) * P]
                    last = tr(to, row(src)[:, k * P:(k + 1) * P], ident[:, :])
                last.then_inc(hT_psum, 1)

            def project(slot, k, pair, columns=((0, HALF), (HALF, SEQ)), signal=True):
                w = [ws[:, slot, part, k * P:(k + 1) * P] for part in range(2)]
                for wp, hp in ((0, 0), (0, 1), (1, 0)):
                    for at, end in columns:
                        last = mm(PP[pair][:, at:end], w[wp], hT[:, hp, k, at:end],
                                  start=(k == 0 and (wp, hp) == (0, 0)), stop=(k == KT - 1 and wp == 1))
                if k == KT - 1 and signal:
                    last.then_inc(chunk_used, 1)
                return last

            def scores(u):
                (first, n), start = keys(u), scores_at(u)
                heads = slice(u % 2 * HD, (u % 2 + 1) * HD)
                for at, end in ((start, min(start + max(n, 256), 512)), (512, start + n)):
                    if at >= end:
                        continue
                    for n_pass, (qp, kp) in enumerate(((0, 0), (0, 1), (1, 0))):
                        last = mm(PP[u % 3][:, at:end], q_parts[qp][heads, u // 2 * P:(u // 2 + 1) * P],
                                  k_parts[kp][heads, first * P + at - start:first * P + end - start],
                                  start=n_pass == 0, stop=n_pass == 2)
                last.then_inc(scores_psum, 1)

            def transpose_p(u):
                _, n = keys(u)
                for j in range(n // P):
                    last = tr(PP[u % 3][:, j * P:(j + 1) * P], s_sb[u % 2][:, j * P:(j + 1) * P], ident[:, :])
                last.then_inc(pT_psum, 1)

            def times_v(u):
                h, (first, n) = u % 2, keys(u)
                for j in range(n // P):
                    last = mm(PP[u % 3][:, OUT_AT:OUT_AT + HD], pT[u % 2][:, j * P:(j + 1) * P],
                              row(V, HD, (first + j) * P + h * HD), start=(j == 0), stop=(j == n // P - 1))
                last.then_inc(o_psum, 1)

            def step(t, s, groups, conv_at, post):
                mine = list(groups)

                def fill(n):
                    for _ in range(min(n, len(mine))):
                        f, k = mine.pop(0)
                        if k == 0:
                            pe.wait_ge(w_split, t * 6 + 4 + f)
                            pe.wait_ge(proj_free, t * 6 + 3 + f)
                        project((3 + f) % 2, k, 3)

                if s == 0:
                    pe.wait_ge(qk_ready, t * 2 + 2)
                if s < UNITS:
                    pe.wait_ge(unit_free, t * UNITS + 1 + max(0, s - 2))
                    if s == 2:
                        pe.wait_ge(v_ready, t * 2 + 2)
                    scores(s)
                if s == 0:
                    fill(1)
                    pe.wait_ge(proj_free, t * 6 + 3)
                    for i in range(NT):
                        last = tr(PP[2][:, i * P:(i + 1) * P], row(VN, P, i * P), ident[:, :])
                    last.then_inc(vT_psum, 1)
                if s == 1:
                    fill(1 if post else 2)
                elif len(mine) > 1 or s >= UNITS:
                    fill(2 if len(mine) == 2 and mine[-1][1] == KT - 1 else 1)
                if s >= 2:
                    pe.wait_ge(pT_act, t * UNITS + s - 1)
                    if s - 2 >= 8:
                        pe.wait_ge(pT_dve, t * 8 + s - 9)
                    bank = PP[(s - 2) % 3]
                    if s == conv_at:
                        pe.wait_ge(conv_sq, t + 1)
                        conv_stats(bank)
                        fill(1)
                    if conv_at and s in (conv_at + 2, conv_at + 3):
                        pe.wait_ge(conv_rs, t + 1)
                        conv_norms(bank, 4 * (s - conv_at - 2), 4)
                    times_v(s - 2)
                if s == 1:
                    pe.wait_ge(exp_done, t * UNITS + s)
                    transpose_p(s - 1)
                if post and s == 1:
                    pe.wait_ge(v_ready, t * 2 + 2)
                    transpose_o(t, 2)
                fill(8)
                if 2 <= s <= UNITS:
                    pe.wait_ge(exp_done, t * UNITS + s)
                    transpose_p(s - 1)
                if post and s == 1:
                    pe.wait_ge(oT_read, t)

            def transpose_o(t, pair):
                pe.wait_ge(o_ready, t)
                for i in range(NT):
                    last = tr(PP[pair][:, i * P:(i + 1) * P], row(CR, P, i * P), ident[:, :])
                last.then_inc(oT_psum, 1)

            def conv_stats(bank):
                for i in range(NT):
                    last = mm(bank[:, 2 * i:2 * i + 2], row(CU, P, i * P), group[:, :], start=True, stop=True)
                return last

            def conv_norms(bank, first, n):
                for b in range(n):
                    last = tr(bank[:, b * P:(b + 1) * P], row(CR, P, (first + b) * P), ident[:, :])
                return last

            def first_pair(f, at, end):
                if at == 0:
                    pe.wait_ge(w_split, f + 1)
                for k in range(KT):
                    project((2, 3, 0)[f], k, (3, 2, 1)[f], ((at, end),), end == SEQ)

            def keep_warm(n):
                for _ in range(n):
                    tr(PP[3][:, HALF:HALF + P], ident[:, :], ident[:, :])

            pe.wait_ge(consts_made, 5)
            for n in range(4):
                keep_warm((20, 0, 0, 0)[n])
                if n == 3:
                    pe.wait_ge(hT_done, 1)
                transpose_h(n, n)
            keep_warm(28)
            pe.wait_ge(hT_done, 4)
            first_pair(0, 0, HALF)
            transpose_h(4, 4)
            transpose_h(5, 5)
            first_pair(1, 0, HALF)
            pe.wait_ge(hT_done, 6)
            transpose_h(6, 6)
            transpose_h(7, 7)
            first_pair(2, 0, HALF)
            pe.wait_ge(hT_done, NT)
            for f in range(3):
                first_pair(f, HALF, SEQ)
            full = [[(s // 3, k) for k in range(8) if k // 3 == s % 3] for s in range(STEPS)]
            late = full[0:3] + [[(1, 0), (1, 1)]] + [[(1, k)] for k in range(2, 8)] + [[(2, k)] for k in range(8)]
            for s in range(2):
                step(0, s, full[s], None, False)
            with pe.Fori(0, PAIRS - 1) as t:
                for s in range(2, STEPS):
                    step(t, s, full[s], CONV_AT, False)
                for s in range(2):
                    step(t + 1, s, full[s], None, True)
            for s in range(2, STEPS):
                step(PAIRS - 1, s, late[s], None, False)

            def out_pair(i):
                return i % 4 if i < 6 else i - 4

            def down(slot, a, tiles, pairs, width, phase, first, last_k, done, signal=True):
                hi, lo = a_slot(a, width, phase)
                for n, tile in enumerate(tiles):
                    pair = PP[pairs[n]]
                    if first:
                        first(n)
                    for part, (ap, wp) in enumerate(((hi, 0), (hi, 1), (lo, 0))):
                        for half in range(2):
                            last = mm(pair[:, half * 512:(half + 1) * 512], ap[:, tile * P:(tile + 1) * P],
                                      ws[:, slot, wp, half * 512:(half + 1) * 512],
                                      start=(first is not None and part == 0), stop=(last_k and part == 2))
                    if last_k and n < len(tiles) - 1:
                        last.then_inc(done, 1)
                if signal:
                    last.then_inc(chunk_used, 1)
                return last

            pe.wait_ge(unit_free, PAIRS * UNITS + 1)
            before = {12: 0, 13: 1, 14: 2, 21: 3, 22: 4}
            for c in range(len(PASSES) * KT):
                p, m = c // KT, c % KT
                tiles = PASSES[p]
                if c in before:
                    i = before[c]
                    pe.wait_ge(y_copied, 3 if i < 3 else 6)
                    if i in (1, 2):
                        pe.wait_ge(hT_done, NT + i)
                    transpose_h(NT + i, H_O[i % 2])
                if c == 2:
                    pe.wait_ge(proj_free, OUT0)
                    transpose_o(PAIRS, 3)
                if c == 3:
                    pe.wait_ge(oT_read, PAIRS)
                    pe.wait_ge(conv_sq, PAIRS)
                    conv_stats(PP[3]).then_inc(conv_stat, 1)
                if c == 6:
                    pe.wait_ge(conv_rs, PAIRS)
                    conv_norms(PP[3], 0, NT).then_inc(conv_norm, 1)
                pe.wait_ge(w_split, OUT0 + LOAD[c] + 1)
                pe.wait_ge(a_split, c + 1)

                def begin(n, p=p):
                    if p == 1 and n == 0:
                        pe.wait_ge(mix_done, 1)
                    if p == 1 and n >= 1:
                        pe.wait_ge(y_copied, n)
                    if p == 2 and n == 0:
                        pe.wait_ge(hT_done, NT + 3)
                    if p == 2 and n == 1:
                        pe.wait_ge(y_copied, 4)
                down(out_slot(c), mix_slot(c), range(len(tiles)), [out_pair(i) for i in tiles], len(tiles) * P, "mix",
                     begin if m == 0 else None, m == KT - 1, y_psum)

            def first_tiles(c, at, end):
                if at == 0:
                    pe.wait_ge(w_split, FIN0 + c + 1)
                for k in range(KT):
                    project(ffn_slot(c), k, c, ((at, end),), end == SEQ)

            pe.wait_ge(hT_done, NT + 4)
            first_tiles(0, 0, HALF)
            pe.wait_ge(hT_done, NT + 5)
            transpose_h(NT + 5, H_O[1])
            first_tiles(1, 0, HALF)
            pe.wait_ge(y_copied, NT)
            first_tiles(2, 0, HALF)
            transpose_h(NT + 6, H_O[0])
            first_tiles(3, 0, HALF)
            pe.wait_ge(hT_done, NT + 6)
            transpose_h(NT + 7, H_O[1])
            pe.wait_ge(hT_done, NT + 7)
            first_tiles(2, HALF, 6 * P)
            pe.wait_ge(hT_done, 2 * NT)
            for c in range(4):
                first_tiles(c, 6 * P if c == 2 else HALF, SEQ)

            def ffn_in(j, par, last=False):
                pe.wait_ge(act_done, j - 1)
                for gu in range(2):
                    pe.wait_ge(w_split, j * 2 + FIN0 + gu + 1)
                    for k in range(KT):
                        done = project(ffn_slot(2 * par + gu), k, 2 * par + gu)
                        if last and gu == 1 and k < 4:
                            done.then_inc(hT_free, 1)

            with pe.Fori(1, NF // 2 - 1) as jj:
                for par in range(2):
                    ffn_in(jj * 2 + par, par)
            ffn_in(NF - 2, 0)
            ffn_in(NF - 1, 1, True)

            def ffn_out(g, c, hf, first, last_k):
                pe.wait_ge(w_split, g + 1)
                pe.wait_ge(a_split, g - FOUT0 + NOUT + 1)

                def begin(n):
                    if hf == 0:
                        pe.wait_ge(act_done, NF - 1 if n < 2 else NF)
                    else:
                        pe.wait_ge(f_copied, n + 1)
                down(ffn_slot(c), c % 4, range(4), range(4), 512, "ffn", begin if first else None, last_k, f_psum)

            for c in range(4):
                ffn_out(FOUT0 + c, c, 0, c == 0, False)
            with pe.Fori(1, 5) as r:
                for c in range(4):
                    ffn_out(r * 4 + FOUT0 + c, c, 0, False, False)
            for c in range(20, 28):
                hf = c // NF
                ffn_out(FOUT0 + c, c, hf, c % NF == 0, c % NF == NF - 1)
            with pe.Fori(0, 3) as r:
                for c in range(28, 32):
                    ffn_out(r * 4 + FOUT0 + c, c, 1, False, False)
            for n in range(4):
                for c in range(40, 44):
                    if n == 0:
                        pe.wait_ge(w_split, FOUT0 + c + 1)
                        pe.wait_ge(a_split, NOUT + c + 1)
                    last = down(ffn_slot(c), c % 4, (n,), (n,), 512, "ffn", None, c == 43, f_psum, False)
                last.then_inc(f_psum, 1)

        @block.scalar
        def _(act):
            go = nc.scalar.activation

            def high(g, slot, raw_slot, wait_used):
                act.wait_ge(raw_landed[raw_slot], (g // 2) * 16 + 16 if isinstance(g, int) else g)
                if wait_used is not None:
                    act.wait_ge(chunk_used, wait_used)
                go(ws[:, slot, 0, :], raw[:, raw_slot, :], ACT.Copy).then_inc(w_hi, 1)

            def high_r(landed, slot, raw_slot, wait_used):
                act.wait_ge(raw_landed[raw_slot], landed)
                act.wait_ge(chunk_used, wait_used)
                go(ws[:, slot, 0, :], raw[:, raw_slot, :], ACT.Copy).then_inc(w_hi, 1)

            last_junk = []

            def square(src, dst, acc, done):
                if last_junk:
                    act.wait_ge(*last_junk[-1])
                go(dst, src, ACT.Square, accum_out=acc).then_inc(done[0], 1)
                last_junk.append(done)

            def high_hT(n):
                act.wait_ge(hT_psum, n + 1)
                for src, dst in h_parts(0, n):
                    last = go(dst, src, ACT.Copy)
                last.then_inc(hT_hi, 1)

            def sq_x(n):
                act.wait_ge(x_landed[n], 16)
                square(row(n), row(JUNK), ssq[:, n:n + 1], (x_sq, n + 1))

            for n in range(4):
                sq_x(n)
            high_hT(0), high_hT(1), sq_x(4), high_hT(2), sq_x(5), high_hT(3)
            high(0, 2, 0, None)
            sq_x(6), sq_x(7)
            high(1, 3, 1, None)
            high_hT(4), high_hT(5)
            high(2, 0, 0, None)
            high_hT(6), high_hT(7)
            high(3, 1, 1, None)
            act.wait_ge(bias_landed, 32)
            for h in range(4):
                go(bias[:, (4 + h) * BAND:(5 + h) * BAND], turned[:, h, ::-1], ACT.Copy).then_inc(bias_turned, 1)
            scale = HD ** -0.5
            act.wait_ge(chunk_used, 1)
            go(q_parts[0], PP[3], ACT.Copy, scale=scale).then_inc(qk_high, 1)
            act.wait_ge(chunk_used, 2)
            go(k_parts[0], PP[2], ACT.Copy).then_inc(qk_high, 1)
            act.wait_ge(proj_free, 2)
            act.wait_ge(chunk_used, 3)
            go(row(VN), PP[1], ACT.Copy).then_inc(proj_free, 1)

            def step(t, s, evac, splits, more):
                if s < UNITS:
                    act.wait_ge(biased, t * UNITS + s + 1)
                    _, n = keys(s)
                    go(s_sb[s % 2][:, 0:n], s_sb[s % 2][:, 0:n], ACT.Exp, bias=nmax[:, s % 2:s % 2 + 1],
                       accum_out=lsum[:, s:s + 1]).then_inc(exp_done, 1)
                if s == CONV_AT - 1 and more:
                    square_conv(t, 4)
                if s == 0:
                    act.wait_ge(vT_psum, t + 1)
                    go(row(V, 512), PP[2][:, 0:512], ACT.Copy).then_inc(v_ready, 1)
                if s in evac:
                    f = evac[s]
                    dst = {0: CV, 2: QN, 4: KN, 5: VN}[f]
                    act.wait_ge(chunk_used, t * 6 + 4 + f)
                    go(row(dst), PP[3], ACT.Copy).then_inc(proj_free, 1)
                if 1 <= s <= UNITS:
                    u = s - 1
                    _, n = keys(u)
                    act.wait_ge(pT_psum, t * UNITS + u + 1)
                    if u >= 2:
                        act.wait_ge(o_psum, t * UNITS + u - 1)
                    go(pT[u % 2][:, 0:min(n, 512)], PP[u % 3][:, 0:min(n, 512)], ACT.Copy).then_inc(pT_act, 1)
                if s in splits:
                    g = 3 + splits[s]
                    high_r((t * 3 + g // 2) * 16 + 16, g % 2, g % 2, t * 6 + g - 1)
                if s >= 2:
                    u = s - 2
                    act.wait_ge(unit_free, t * UNITS + u + 2)
                    if u:
                        act.wait_ge(o_sq, t * UNITS + u)
                    go(sq_junk[:, :], o_raw[:, u // 2, (u % 2) * HD:(u % 2 + 1) * HD], ACT.Square,
                       scale=HD ** -0.5, accum_out=osq[:, u:u + 1]).then_inc(o_sq, 1)
                if s == CONV_AT + 1 and more:
                    spread_conv(t)
                if s == UNITS - 1 and more:
                    act.wait_ge(scores_psum, t * UNITS + UNITS)
                    act.wait_ge(proj_free, t * 6 + 3 + 3)
                    go(q_parts[0], row(QN), ACT.Copy, scale=scale).then_inc(qk_high, 1)
                    act.wait_ge(proj_free, t * 6 + 3 + 5)
                    go(k_parts[0], row(KN), ACT.Copy).then_inc(qk_high, 1)

            def spread_conv(t):
                act.wait_ge(conv_factors, t + 1)
                go(row(CR).rearrange("p (g d) -> p g d", d=HD),
                   crs[:, :].rearrange("p (g o) -> p g o", o=1).broadcast_to([P, 16, HD]), ACT.Copy
                   ).then_inc(conv_rs, 1)

            def square_conv(t, chunks):
                act.wait_ge(proj_free, t * 6 + 3 + chunks)
                go(row(CU), row(CV), ACT.Square).then_inc(conv_sq, 1)

            evac, splits = {2: 0, 8: 2, 14: 4, 17: 5}, {1: 1, 3: 2, 6: 3, 10: 4, 12: 5, 15: 6}
            for s in range(2):
                step(0, s, evac, splits, False)
            with act.Fori(0, PAIRS - 1) as t:
                for s in range(2, STEPS):
                    step(t, s, evac, splits, True)
                for s in range(2):
                    step(t + 1, s, evac, splits, False)

            def split_out(c):
                if fresh(c):
                    split_out_w(c)
                split_out_a(c)

            def split_out_w(c):
                g = OUT0 + LOAD[c]
                act.wait_ge(raw_landed[g % 2], (g // 2) * 16 + 16)
                act.wait_ge(chunk_used, OUT0 - 1 if c < 2 else OUT0 + c - 2)
                go(ws[:, out_slot(c), 0, :], raw[:, g % 2, :], ACT.Copy).then_inc(w_hi, 1)

            def split_out_a(c):
                tiles = PASSES[c // KT]
                width = len(tiles) * P
                if c >= 2:
                    last = c - 2 if c <= 2 * KT else max(c - 4, 2 * KT - 2 + (c - 2 * KT) // 2)
                    act.wait_ge(chunk_used, OUT0 + last + 1)
                if c == 6:
                    act.wait_ge(oT_read, PAIRS)
                if c == 7:
                    act.wait_ge(mix_done, 1)
                hi, _ = a_slot(mix_slot(c), width, "mix")
                go(hi, row(yT + ROWS[c], width, tiles[0] * P), ACT.Copy).then_inc(a_hi, 1)

            for s in range(2, STEPS):
                step(PAIRS - 1, s, {2: 0}, {3: 2}, False)
                if s == 10:
                    split_out_w(0)
                if s == UNITS - 1:
                    act.wait_ge(scores_psum, PAIRS * UNITS)
                    split_out_w(1)
                    split_out_a(0)
                if s == UNITS:
                    split_out_a(1)
            square_conv(PAIRS - 1, 3)

            def copy_y(i):
                done, value = {0: (y_psum, 1), 1: (y_psum, 2), 2: (chunk_used, OUT0 + KT),
                               3: (y_psum, 3), 4: (y_psum, 4), 5: (chunk_used, OUT0 + 2 * KT),
                               6: (y_psum, 5), 7: (chunk_used, OUT0 + 3 * KT)}[i]
                act.wait_ge(done, value)
                if i >= 3:
                    act.wait_ge(x2_ready, i - 2)
                pair = i % 4 if i < 6 else i - 4
                go(row(YS[i % 3]), PP[pair], ACT.Copy).then_inc(y_copied, 1)

            def sq_y(i):
                act.wait_ge(y_copied, i + 1)
                square(row(YS[i % 3]), row(JUNK), ssq[:, 8 + i:9 + i], (y_sq, i + 1))

            def sq_x2(i):
                act.wait_ge(x2_ready, i + 1)
                act.dma_start(x2_d[i * P:(i + 1) * P, :], row(XS[i % 4])).then_inc(x2_stored[i % 4], 16)
                square(row(XS[i % 4]), row(JUNK), ssq[:, 16 + i:17 + i], (x2_sq, i + 1))

            tasks = {7: [(copy_y, 0), (sq_y, 0)], 8: [(copy_y, 1), (copy_y, 2), (sq_y, 1), (sq_y, 2)],
                     9: [(sq_x2, 0)], 10: [(sq_x2, 1)], 12: [(high_hT, NT), (sq_x2, 2)],
                     13: [(high_hT, NT + 1)], 14: [(high_hT, NT + 2)],
                     15: [(copy_y, 3), (sq_y, 3)], 16: [(copy_y, 4), (copy_y, 5), (sq_y, 4)], 17: [(sq_y, 5)],
                     18: [(sq_x2, 3)], 19: [(sq_x2, 4)], 20: [], 21: [(high_hT, NT + 3), (sq_x2, 5)], 22: [(high_hT, NT + 4)],
                     23: []}
            for c in range(1, NOUT):
                for ahead in split_ahead(c):
                    split_out(ahead)
                if c == 4:
                    act.wait_ge(oT_psum, PAIRS)
                    spread_conv(PAIRS - 1)
                for task, i in tasks.get(c, ()):
                    task(i)
            high(FIN0, ffn_slot(0), 0, FIN0 + AGAIN - 2)
            high(FIN0 + 1, ffn_slot(1), 1, FIN0 + AGAIN - 1)
            copy_y(6), sq_y(6), copy_y(7), sq_y(7), high_hT(NT + 5)
            high(FIN0 + 2, ffn_slot(2), 0, FIN0 + AGAIN)
            sq_x2(6)
            high(FIN0 + 3, ffn_slot(3), 1, FIN0 + AGAIN)
            sq_x2(7), high_hT(NT + 6), high_hT(NT + 7)

            def ffn_in(j, landed, par, more=True):
                act.wait_ge(chunk_used, j * 2 + FIN0 + AGAIN + 1)
                if not isinstance(j, int) or j >= 2:
                    act.wait_ge(act_done, j - 1)
                go(sil[par], PP[2 * par], ACT.Silu).then_inc(silu_done, 1)
                if more:
                    for gu in range(2):
                        high_r(landed, ffn_slot(2 * par + gu), gu, j * 2 + FIN0 + AGAIN + 1 + gu)

            for j in range(2):
                ffn_in(j, (FIN0 // 2 + j + 2) * 16 + 16, j)
            with act.Fori(1, NF // 2 - 1) as jj:
                for par in range(2):
                    ffn_in(jj * 2 + par, (jj * 2 + FIN0 // 2 + par + 2) * 16 + 16, par)
            ffn_in(NF - 2, (FIN0 // 2 + NF) * 16 + 16, 0)
            ffn_in(NF - 1, None, 1, False)

            def ffn_high(g, landed, c, hf, f, with_w=True, between=()):
                if isinstance(g, int) and g < FOUT0 + 4:
                    act.wait_ge(hT_free, c + 1)
                else:
                    act.wait_ge(chunk_used, g + AGAIN - 3)
                hi, _ = a_slot(c % 4, 512, "ffn")
                go(hi, arena[:, bass.ds(f * SEQ + hf * HALF, HALF)], ACT.Copy).then_inc(a_hi, 1)
                for n in between:
                    copy_f(n)
                if with_w:
                    high_r(landed, ffn_slot(c + 2), c % 2, g + AGAIN - 1)

            def copy_f(n):
                act.wait_ge(*((f_psum, n + 1) if n < 3 else (chunk_used, FOUT0 + AGAIN + NF)))
                go(yt[n], PP[n].rearrange("p (a b) -> p a b", a=2), ACT.Copy).then_inc(f_copied, 1)

            def sq_f(i):
                if i < 4:
                    act.wait_ge(f_copied, i + 1)
                    square(yt[i], junk3, ssq[:, 24 + i:25 + i], (f_sq, i + 1))
                else:
                    act.wait_ge(f_psum, i)
                    square(PP[i - 4], sil[1], ssq[:, 24 + i:25 + i], (f_sq, i + 1))

            junk3 = sil[1].rearrange("p (a b) -> p a b", a=2)

            def landed_of(c):
                return ((FOUT0 + 2 + c) // 2) * 16 + 16

            for c in range(4):
                ffn_high(FOUT0 + c, landed_of(c), c, 0, c)
            with act.Fori(1, 5) as r:
                for c in range(4):
                    ffn_high(r * 4 + FOUT0 + c, r * 32 + landed_of(c), c, 0, r * 4 + c)
            for c in range(20, 28):
                if c == 24:
                    copy_f(3)
                ffn_high(FOUT0 + c, landed_of(c), c, c // NF, c % NF, between=(0, 1, 2) if c == 23 else ())
                if c >= 24:
                    sq_f(c - 24)
            with act.Fori(0, 3) as r:
                for c in range(28, 32):
                    ffn_high(r * 4 + FOUT0 + c, r * 32 + landed_of(c), c, 1, r * 4 + c - NF)
            for c in range(40, 44):
                ffn_high(FOUT0 + c, landed_of(c), c, 1, c - NF, c < 42)
            for i in range(4, NT):
                sq_f(i)

        @block.vector
        def _(dve):
            chain = Chain(dve, dve_seq)
            ts, tt, stt = nc.vector.tensor_scalar, nc.vector.tensor_tensor, nc.vector.scalar_tensor_tensor

            def rsqrt(dst, v, n):
                y, a = dst, newt[:, 0:n]
                chain(ts(y.bitcast(I32), v.bitcast(I32), -0.5, float(0x5F3759DF), ALU.mult, ALU.add))
                for _ in range(3):
                    chain(tt(a, y, y, ALU.mult))
                    chain(stt(a, a, -0.5, v, ALU.mult, ALU.mult))
                    chain(stt(y, a, 1.5, y, ALU.add, ALU.mult))

            def low(n_hi, slot, raw_slot):
                dve.wait_ge(w_hi, n_hi)
                tt(ws[:, slot, 1, :], raw[:, raw_slot, :], ws[:, slot, 0, :].bitcast(F32),
                   ALU.subtract).then_inc(w_split, 1)

            def low_hT(n):
                dve.wait_ge(hT_hi, n + 1)
                for (src, dst), (_, hi) in zip(h_parts(1, n), h_parts(0, n)):
                    last = tt(dst, src, hi.bitcast(F32), ALU.subtract)
                last.then_inc(hT_done, 1)

            dve.wait_ge(gpre_landed, 16)

            def norm_x(n):
                if n >= 2:
                    dve.wait_ge(x_rs, n // 2)
                stt(row(n), row(n), xrs[:, n:n + 1], row(GPRE), ALU.mult, ALU.mult).then_inc(h_ready, 1)

            dve.wait_ge(x_sq, 2)
            chain(ts(var[:, 0:2], ssq[:, 0:2], 1.0 / D, EPS, ALU.mult, ALU.add))
            rsqrt(xrs[:, 0:2], var[:, 0:2], 2)
            norm_x(0), norm_x(1), low_hT(0), norm_x(2), low_hT(1), norm_x(3), low_hT(2), low_hT(3)
            low(1, 2, 0)
            norm_x(4), norm_x(5)
            low(2, 3, 1)
            norm_x(6), norm_x(7), low_hT(4), low_hT(5)
            low(3, 0, 0)
            low_hT(6), low_hT(7)
            low(4, 1, 1)
            dve.wait_ge(hT_done, NT)
            dve.wait_ge(const_landed, 48)
            nc.vector.memset(gate[:, :], 0.0).then_inc(unit_free, 1)
            dve.wait_ge(qk_high, 2)
            scale = HD ** -0.5
            stt(q_parts[1], PP[3], scale, q_parts[0].bitcast(F32), ALU.mult, ALU.subtract).then_inc(proj_free, 1)
            tt(k_parts[1], PP[2], k_parts[0].bitcast(F32), ALU.subtract).then_inc(proj_free, 1)
            dve.wait_ge(proj_free, 2)
            nc.vector.memset(nmax[:, :], 0.0).then_inc(qk_ready, 2)
            dve.wait_ge(bias_ready, 2)

            def is_last(t):
                return isinstance(t, int) and t == PAIRS - 1

            def step(t, s, evac, taps, splits, conv_at, more, post):
                if s == 0 and post:
                    chain(stt(o_eps[:, :], lsum[:, :], EPS, lsum[:, :], ALU.mult, ALU.mult))
                if s == 2:
                    chain(nc.vector.tensor_copy(cur[:, :], params[:, :, :].rearrange("p t c -> p (t c)")[
                        :, bass.ds(t * 5, 5)]))
                if s in evac and is_last(t):
                    read_chunk(t, evac[s])
                if s == 1 and post:
                    o_scale(t)
                if s < UNITS:
                    _, n = keys(s)
                    dve.wait_ge(scores_psum, t * UNITS + s + 1)
                    if s >= 2:
                        dve.wait_ge(pT_psum, t * UNITS + s - 1)
                    if s >= 1:
                        dve.wait_ge(biased, t * UNITS + s)
                    nc.vector.memset(gate[:, :], 0.0)
                    at = scores_at(s)
                    b = bias[:, (s % 2 + 1) * BAND - n:(s % 2 + 1) * BAND]
                    chain(nc.vector.tensor_tensor_reduce(
                        out=s_sb[s % 2][:, 0:n], in0=PP[s % 3][:, at:at + n], in1=b, scale=1.0, scalar=-3e38,
                        op0=ALU.add, op1=ALU.max, accum_out=omax[:, :]))
                    ts(nmax[:, s % 2:s % 2 + 1], omax[:, :], -1.0, None, ALU.mult).then_inc(biased, 1)
                if s == 0 and post:
                    o_norm(t)
                if s == 0:
                    dve.wait_ge(vT_psum, t + 1)
                    nc.vector.tensor_copy(row(V, 512, 512), PP[2][:, 512:1024]).then_inc(v_ready, 1)
                if s >= 2:
                    u = s - 2
                    bank = PP[u % 3]
                    dve.wait_ge(o_psum, t * UNITS + u + 1)
                    if s == conv_at:
                        ts(var[:, :], bank[:, 0:16], 1.0 / HD, EPS, ALU.mult, ALU.add).then_inc(conv_var, 1)
                    if conv_at and s in (conv_at + 2, conv_at + 3):
                        at = 512 * (s - conv_at - 2)
                        chain(stt(arena[:, bass.ds(t * SEQ + at, 512)], bank[:, 0:512], cur[:, 3:4],
                                  row(CV, 512, at), ALU.mult, ALU.mult))
                    nc.vector.tensor_copy(o_raw[:, u // 2, (u % 2) * HD:(u % 2 + 1) * HD],
                                          bank[:, OUT_AT:OUT_AT + HD]).then_inc(unit_free, 1)
                if s in evac and not is_last(t):
                    read_chunk(t, evac[s])
                if s in taps:
                    n = taps.index(s)
                    if n == 0:
                        chain(ts(row(CV), cu[:, 0:SEQ], cur[:, 0:1], None, ALU.mult))
                    else:
                        chain(stt(row(CV), cu[:, n:n + SEQ], cur[:, n:n + 1], row(CV), ALU.mult, ALU.add))
                if is_last(t):
                    if s in splits:
                        split_in(t, splits[s])
                    if s in (11, 16):
                        g = OUT0 + s // 16
                        low(g + 1, out_slot(g - OUT0), g % 2)
                    if s in (16, 17):
                        split_out_a(s - 16)
                if 9 <= s <= UNITS:
                    u = s - 1
                    dve.wait_ge(pT_psum, t * UNITS + u + 1)
                    dve.wait_ge(o_psum, t * UNITS + u - 1)
                    nc.vector.tensor_copy(pT[u % 2][:, 512:BAND], PP[u % 3][:, 512:BAND]).then_inc(pT_dve, 1)
                if not is_last(t) and s in splits and not (s == 1 and post):
                    split_in(t, splits[s])
                if s == 1 and post:
                    o_finish(t, PP[2])
                    split_in(t, splits[s])
                if s == UNITS - 1 and more:
                    dve.wait_ge(qk_high, t * 2 + 3)
                    stt(q_parts[1], row(QN), scale, q_parts[0].bitcast(F32), ALU.mult, ALU.subtract
                        ).then_inc(qk_ready, 1)
                if s == UNITS and more:
                    dve.wait_ge(qk_high, t * 2 + 4)
                    tt(k_parts[1], row(KN), k_parts[0].bitcast(F32), ALU.subtract).then_inc(qk_ready, 1)
                if s == STEPS - 1 and more:
                    dve.wait_ge(biased, t * UNITS + UNITS)
                    chain(nc.vector.tensor_copy(bias[:, 0:2 * BAND],
                                                bias[:, bass.ds((t + 1) * 2 * BAND, 2 * BAND)]))

            def split_in(t, f):
                g = 3 + f
                low(t * 6 + g + 1, g % 2, g % 2)

            def read_chunk(t, f):
                dve.wait_ge(chunk_used, t * 6 + 4 + f)
                if f == 1:
                    nc.vector.memset(cu[:, 0:TAPS - 1], 0.0)
                    tt(cu[:, TAPS - 1:TAPS - 1 + SEQ], PP[3], row(CV), ALU.mult).then_inc(proj_free, 1)
                    dve.wait_ge(proj_free, t * 6 + 3 + 2)
                else:
                    conv_out(t, f + 1)

            def conv_out(t, chunks):
                tt(row(CV), PP[3], row(CV), ALU.mult).then_inc(proj_free, 1)
                dve.wait_ge(proj_free, t * 6 + 3 + chunks)

            def o_norm(t):
                dve.wait_ge(o_sq, t * UNITS)
                tt(o_eps[:, :], o_eps[:, :], osq[:, :], ALU.add).then_inc(o_var, 1)

            def o_scale(t):
                dve.wait_ge(o_rs, t)
                if not isinstance(t, int):
                    dve.wait_ge(conv_rs, t)
                    dve.wait_ge(o_psum, t * UNITS)
                tt(row(CR).rearrange("p (u d) -> p u d", d=HD),
                   o_raw[:, :, :].rearrange("p i (h d) -> p (i h) d", h=2),
                   rst[:, :].rearrange("p (u o) -> p u o", o=1).broadcast_to([P, UNITS, HD]),
                   ALU.mult).then_inc(o_ready, 1)
                dve.wait_ge(o_ready, t)

            def o_finish(t, pair):
                dve.wait_ge(oT_psum, t)
                ts(arena[:, bass.ds((t + PAIRS - 1) * SEQ, SEQ)], pair, cur[:, 4:5], None, ALU.mult
                   ).then_inc(oT_read, 1)
                dve.wait_ge(oT_read, t)


            def split_out(c):
                g = OUT0 + LOAD[c]
                if fresh(c):
                    low(g + 1, out_slot(c), g % 2)
                split_out_a(c)

            def split_out_a(c):
                tiles = PASSES[c // KT]
                width = len(tiles) * P
                hi, lo = a_slot(mix_slot(c), width, "mix")
                dve.wait_ge(a_hi, c + 1)
                tt(lo, row(yT + ROWS[c], width, tiles[0] * P), hi.bitcast(F32), ALU.subtract
                   ).then_inc(a_split, 1)

            args = ({5: 1, 11: 3}, (6, 8, 9), {1: 1, 4: 2, 7: 3, 10: 4, 12: 5, 15: 6}, CONV_AT)
            for s in range(2):
                step(0, s, *args, False, False)
            with dve.Fori(0, PAIRS - 1) as t, chain.loop(t, PAIRS - 1, 24):
                for s in range(2, STEPS):
                    step(t, s, *args, True, False)
                for s in range(2):
                    step(t + 1, s, *args, False, True)

            for s in range(2, STEPS):
                step(PAIRS - 1, s, {10: 1}, (12, 13, 14), {4: 2}, None, False, False)
            chain(stt(o_eps[:, :], lsum[:, :], EPS, lsum[:, :], ALU.mult, ALU.mult))
            o_norm(PAIRS)
            dve.wait_ge(chunk_used, OUT0)
            conv_out(PAIRS - 1, 3)

            def norm_y(i):
                dve.wait_ge(y_rs, i + 1)
                y, xs = row(YS[i % 3]), row(XS[i % 4])
                chain(stt(y, y, yrs[:, i:i + 1], row(GPM), ALU.mult, ALU.mult))
                dve.wait_ge(xr_landed[i % 4], 16 * (i // 4) + 16)
                tt(xs, y, xs, ALU.add).then_inc(x2_ready, 1)

            def norm_x2(i):
                dve.wait_ge(x2_rs, i + 1)
                if i >= 2:
                    dve.wait_ge(hT_psum, NT + i - 1)
                stt(row(H_O[i % 2]), row(XS[i % 4]), x2rs[:, i:i + 1], row(GPF), ALU.mult, ALU.mult
                    ).then_inc(h_ready, 1)

            def conv_last_stats(_):
                dve.wait_ge(conv_stat, 1)
                ts(var[:, :], PP[3][:, 0:16], 1.0 / HD, EPS, ALU.mult, ALU.add).then_inc(conv_var, 1)

            def conv_last(_):
                dve.wait_ge(conv_norm, 1)
                stt(row(PAIRS - 1), PP[3], cur[:, 3:4], row(CV), ALU.mult, ALU.mult).then_inc(mix_done, 1)
                dve.wait_ge(mix_done, 1)

            def attn_last(_):
                o_finish(PAIRS, PP[3])

            tasks = {1: [(attn_last, 0)], 3: [(conv_last_stats, 0)], 5: [(conv_last, 0)],
                     8: [(norm_y, 0)], 9: [(norm_y, 1)], 10: [(norm_x2, 0)], 11: [(norm_y, 2)],
                     12: [(norm_x2, 1), (low_hT, NT)], 13: [(norm_x2, 2), (low_hT, NT + 1)],
                     14: [(low_hT, NT + 2)], 16: [(norm_y, 3)], 17: [(norm_y, 4)], 18: [(norm_x2, 3)],
                     19: [(norm_y, 5)], 20: [(norm_x2, 4)],
                     21: [(low_hT, NT + 3)], 22: [(low_hT, NT + 4), (norm_x2, 5)], 23: []}
            for c in range(1, NOUT):
                for ahead in split_ahead(c):
                    split_out(ahead)
                if c == 1:
                    o_scale(PAIRS)
                if c == KT:
                    dve.wait_ge(gmix_landed, 32)
                for task, i in tasks.get(c, ()):
                    task(i)
            low(FIN0 + 1, ffn_slot(0), 0)
            low(FIN0 + 2, ffn_slot(1), 1)
            norm_y(6)
            low_hT(NT + 5)
            low(FIN0 + 3, ffn_slot(2), 0)
            norm_x2(6), norm_y(7)
            low(FIN0 + 4, ffn_slot(3), 1)
            low_hT(NT + 6), norm_x2(7), low_hT(NT + 7)
            for n in range(4):
                dve.wait_ge(x2_stored[n], 16 * (NT // 4))

            def ffn_in(j, par, more=True):
                if more:
                    low(j * 2 + FIN0 + 5, ffn_slot(2 * par), 0)
                dve.wait_ge(silu_done, j + 1)
                dve.wait_ge(chunk_used, j * 2 + FIN0 + AGAIN + 2)
                tt(arena[:, bass.ds(j * SEQ, SEQ)], sil[par], PP[2 * par + 1], ALU.mult).then_inc(act_done, 1)
                if more:
                    low(j * 2 + FIN0 + 6, ffn_slot(2 * par + 1), 1)

            for j in range(2):
                ffn_in(j, j)
            with dve.Fori(1, NF // 2 - 1) as jj:
                for par in range(2):
                    ffn_in(jj * 2 + par, par)
            ffn_in(NF - 2, 0)

            def ffn_low(g, c, hf, f, with_w=True):
                hi, lo = a_slot(c % 4, 512, "ffn")
                dve.wait_ge(a_hi, g - FOUT0 + NOUT + 1)
                tt(lo, arena[:, bass.ds(f * SEQ + hf * HALF, HALF)], hi.bitcast(F32), ALU.subtract
                   ).then_inc(a_split, 1)
                if with_w:
                    low(g + 3, ffn_slot(c + 2), c % 2)

            def norm_f(i):
                n, hf = i % 4, i // 4
                dve.wait_ge(f_sq, i + 1)
                chain(ts(var[:, 0:1], ssq[:, 24 + i:25 + i], 1.0 / D, EPS, ALU.mult, ALU.add))
                rsqrt(rst[:, 0:1], var[:, 0:1], 1)
                if hf:
                    dve.wait_ge(out_stored[n], 16)
                y = PP[n].rearrange("p (a b) -> p a b", a=2) if hf else yt[n]
                gain = sil[0].rearrange("p (a b) -> p a b", a=2)
                dve.wait_ge(x2_landed[n], 16 * hf + 16)
                for part in (slice(0, 1), slice(1, 2)) if i == NT - 1 else (slice(0, 2),):
                    chain(stt(yt[n][:, part], y[:, part], rst[:, 0:1], gain[:, part], ALU.mult, ALU.mult))
                    tt(yt[n][:, part], yt[n][:, part], x2t[n][:, part], ALU.add).then_inc(out_ready, 1)

            dve.wait_ge(act_done, NF - 1)
            ffn_low(FOUT0, 0, 0, 0)
            ffn_low(FOUT0 + 1, 1, 0, 1, False)
            ffn_in(NF - 1, 1, False)
            low(FOUT0 + 4, ffn_slot(3), 1)
            dve.wait_ge(act_done, NF)
            for c in range(2, 4):
                ffn_low(FOUT0 + c, c, 0, c)
            with dve.Fori(1, 5) as r:
                for c in range(4):
                    ffn_low(r * 4 + FOUT0 + c, c, 0, r * 4 + c)
            for c in range(20, 28):
                ffn_low(FOUT0 + c, c, c // NF, c % NF)
                if c == 24:
                    dve.wait_ge(gffn_landed, 16)
                if c >= 24:
                    norm_f(c - 24)
            with dve.Fori(0, 3) as r:
                for c in range(28, 32):
                    ffn_low(r * 4 + FOUT0 + c, c, 1, r * 4 + c - NF)
            for c in range(40, 44):
                ffn_low(FOUT0 + c, c, 1, c - NF, c < 42)
            for i in range(4, NT):
                norm_f(i)


_INS = ["x", "w_in", "w_conv", "rel_bias", "g_conv_out", "g_attn_out", "w_out", "g_pre_mix", "g_post_mix",
        "g_pre_ffn", "g_post_ffn", "w_ffn_in", "w_ffn_out"]


def kernel(**inputs):
    import numpy as np
    import concourse.bacc as bacc
    from concourse.bass_utils import run_bass_kernel_spmd

    nc = bacc.Bacc("TRN2", target_bir_lowering=False, num_devices=1)
    arrays, args = {}, []
    for name in _INS:
        a = np.ascontiguousarray(inputs[name])
        arrays[f"in_{name}"] = a
        args.append(nc.dram_tensor(f"in_{name}", a.shape, mybir.dt.from_np(a.dtype), kind="ExternalInput").ap())
    out = nc.dram_tensor("out_0", inputs["x"].shape, F32, kind="ExternalOutput").ap()
    trunk_layer(nc, *args, out)
    return run_bass_kernel_spmd(nc, [arrays], core_ids=[0]).results[0]["out_0"]
```
